# Optimizing a Trainium2 kernel written in Bass

```python
import jax, jax.numpy as jnp
from jax import lax
import numpy as np

D_MODEL = 1024
BATCH = 1
SEQ = 512
DEPTH = 2
DEC_BATCH = 1
DEC_SEQ = 64
PAST_LEN = 128

CHUNK = 64
N_HEADS = 16
HEAD_DIM = D_MODEL // N_HEADS
LEFT_CHUNKS = 8
WINDOW = LEFT_CHUNKS * CHUNK
BAND = (LEFT_CHUNKS + 1) * CHUNK
REL_CLIP = 2 * CHUNK
N_REL = 2 * REL_CLIP + 1
CONV_W = 3
D_FF = 2816
N_CONV = (DEPTH + 1) // 2
N_ATTN = DEPTH // 2
EPS = 1e-6
ATTN_SCALE = HEAD_DIM ** -0.5

kernel_name = "streaming_conv_chunkattn_macaron"

def rmsnorm(x, g):
    xf = x.astype(jnp.float32)
    y = xf * lax.rsqrt(jnp.mean(xf * xf, axis=-1, keepdims=True) + EPS)
    return (y * g.astype(jnp.float32)).astype(x.dtype)

def swiglu(x, w_gate, w_up, w_down):
    return (jax.nn.silu(x @ w_gate) * (x @ w_up)) @ w_down

def depthwise_causal(u_ext, w_dw):
    T = u_ext.shape[1] - (CONV_W - 1)
    return sum(w_dw[k] * u_ext[:, k:k + T] for k in range(CONV_W))

def conv_mixer_prompt(x, w_in, w_dw, w_out):
    b, c, h = jnp.split(x @ w_in, 3, axis=-1)
    u = c * h
    y = depthwise_causal(jnp.pad(u, ((0, 0), (CONV_W - 1, 0), (0, 0))), w_dw)
    return (b * y) @ w_out, u[:, -(CONV_W - 1):]

def conv_mixer_sample(x, conv_state, w_in, w_dw, w_out):
    b, c, h = jnp.split(x @ w_in, 3, axis=-1)
    u_ext = jnp.concatenate([conv_state.astype(x.dtype), c * h], axis=1)
    y = depthwise_causal(u_ext, w_dw)
    return (b * y) @ w_out, u_ext[:, -(CONV_W - 1):]

def split_heads(x, w_qkv):
    bsz, t, _ = x.shape
    q, k, v = jnp.split(x @ w_qkv, 3, axis=-1)
    shp = (bsz, t, N_HEADS, HEAD_DIM)
    return q.reshape(shp), k.reshape(shp), v.reshape(shp)

def rel_bias_lookup(rel_bias, rel):
    return rel_bias[:, jnp.clip(rel, -REL_CLIP, REL_CLIP) + REL_CLIP].astype(jnp.float32)

def attn_mixer_prompt(x, w_qkv, w_o, rel_bias):
    bsz, S, _ = x.shape
    nc = S // CHUNK
    q, k, v = split_heads(x, w_qkv)
    pad_rows = LEFT_CHUNKS * CHUNK
    kp = jnp.pad(k, ((0, 0), (pad_rows, 0), (0, 0), (0, 0)))
    vp = jnp.pad(v, ((0, 0), (pad_rows, 0), (0, 0), (0, 0)))
    qc = jnp.moveaxis(q.reshape(bsz, nc, CHUNK, N_HEADS, HEAD_DIM), 1, 0)
    i = jnp.arange(CHUNK)
    j = jnp.arange(BAND)
    bias = rel_bias_lookup(rel_bias, i[:, None] + pad_rows - j[None, :])

    def one_chunk(args):
        c, qb = args
        kb = lax.dynamic_slice_in_dim(kp, c * CHUNK, BAND, axis=1)
        vb = lax.dynamic_slice_in_dim(vp, c * CHUNK, BAND, axis=1)
        s = jnp.einsum('bqhd,bkhd->bhqk', qb, kb).astype(jnp.float32) * ATTN_SCALE + bias[None]
        valid = (c * CHUNK - pad_rows + j) >= 0
        s = jnp.where(valid[None, None, None, :], s, -jnp.inf)
        p = jax.nn.softmax(s, axis=-1).astype(vb.dtype)
        return jnp.einsum('bhqk,bkhd->bqhd', p, vb)

    o = lax.map(one_chunk, (jnp.arange(nc), qc))
    o = jnp.moveaxis(o, 0, 1).reshape(bsz, S, D_MODEL)
    keep = min(WINDOW, S)
    return o @ w_o, k[:, S - keep:], v[:, S - keep:]

def attn_mixer_sample(x, k_cache, v_cache, w_qkv, w_o, rel_bias):
    bsz, T, _ = x.shape
    R = k_cache.shape[1]
    q, k, v = split_heads(x, w_qkv)
    kk = jnp.concatenate([k_cache.astype(k.dtype), k], axis=1)
    vv = jnp.concatenate([v_cache.astype(v.dtype), v], axis=1)
    qpos = PAST_LEN + jnp.arange(T)
    kpos = jnp.concatenate([PAST_LEN - R + jnp.arange(R), PAST_LEN + jnp.arange(T)])
    bias = rel_bias_lookup(rel_bias, qpos[:, None] - kpos[None, :])
    qc, kc = qpos // CHUNK, kpos // CHUNK
    valid = (kc[None, :] <= qc[:, None]) & (kc[None, :] >= qc[:, None] - LEFT_CHUNKS)
    s = jnp.einsum('bqhd,bkhd->bhqk', q, kk).astype(jnp.float32) * ATTN_SCALE + bias[None]
    s = jnp.where(valid[None, None], s, -jnp.inf)
    p = jax.nn.softmax(s, axis=-1).astype(vv.dtype)
    o = jnp.einsum('bhqk,bkhd->bqhd', p, vv).reshape(bsz, T, D_MODEL)
    return o @ w_o, k, v

def setup_inputs(seed: int = 0) -> dict:
    key = jax.random.key(seed)
    ks = jax.random.split(key, 24)
    cache_rows = min(WINDOW, PAST_LEN)

    def nrm(k, shape, s=1.0):
        return jax.random.normal(k, shape, jnp.float32) * s

    d, f = D_MODEL, D_FF
    return {
        "x_prompt": nrm(ks[0], (BATCH, SEQ, d)),
        "x_sample": nrm(ks[1], (DEC_BATCH, DEC_SEQ, d)),
        "state_conv": nrm(ks[2], (N_CONV, DEC_BATCH, CONV_W - 1, d)),
        "cache_k": nrm(ks[3], (N_ATTN, DEC_BATCH, cache_rows, N_HEADS, HEAD_DIM)),
        "cache_v": nrm(ks[4], (N_ATTN, DEC_BATCH, cache_rows, N_HEADS, HEAD_DIM)),
        "ffn1_norm": 1.0 + nrm(ks[5], (DEPTH, d), 0.01),
        "ffn1_w_gate": nrm(ks[6], (DEPTH, d, f), d ** -0.5),
        "ffn1_w_up": nrm(ks[7], (DEPTH, d, f), d ** -0.5),
        "ffn1_w_down": nrm(ks[8], (DEPTH, f, d), f ** -0.5),
        "mix_norm": 1.0 + nrm(ks[9], (DEPTH, d), 0.01),
        "conv_w_in": nrm(ks[10], (N_CONV, d, 3 * d), d ** -0.5),
        "conv_w_dw": nrm(ks[11], (N_CONV, CONV_W, d), CONV_W ** -0.5),
        "conv_w_out": nrm(ks[12], (N_CONV, d, d), d ** -0.5),
        "attn_w_qkv": nrm(ks[13], (N_ATTN, d, 3 * d), d ** -0.5),
        "attn_w_o": nrm(ks[14], (N_ATTN, d, d), d ** -0.5),
        "attn_rel_bias": nrm(ks[15], (N_ATTN, N_HEADS, N_REL), 0.5),
        "ffn2_norm": 1.0 + nrm(ks[16], (DEPTH, d), 0.01),
        "ffn2_w_gate": nrm(ks[17], (DEPTH, d, f), d ** -0.5),
        "ffn2_w_up": nrm(ks[18], (DEPTH, d, f), d ** -0.5),
        "ffn2_w_down": nrm(ks[19], (DEPTH, f, d), f ** -0.5),
        "final_norm": 1.0 + nrm(ks[20], (d,), 0.01),
    }

def reference(x_prompt, x_sample, state_conv, cache_k, cache_v,
              ffn1_norm, ffn1_w_gate, ffn1_w_up, ffn1_w_down,
              mix_norm, conv_w_in, conv_w_dw, conv_w_out,
              attn_w_qkv, attn_w_o, attn_rel_bias,
              ffn2_norm, ffn2_w_gate, ffn2_w_up, ffn2_w_down,
              final_norm):
    xp, xs = x_prompt, x_sample
    conv_p, conv_s, kp_l, vp_l, ks_l, vs_l = [], [], [], [], [], []
    for l in range(DEPTH):
        xp = xp + 0.5 * swiglu(rmsnorm(xp, ffn1_norm[l]), ffn1_w_gate[l], ffn1_w_up[l], ffn1_w_down[l])
        xs = xs + 0.5 * swiglu(rmsnorm(xs, ffn1_norm[l]), ffn1_w_gate[l], ffn1_w_up[l], ffn1_w_down[l])
        hp, hs = rmsnorm(xp, mix_norm[l]), rmsnorm(xs, mix_norm[l])
        j = l // 2
        if l % 2 == 0:
            mp, st_p = conv_mixer_prompt(hp, conv_w_in[j], conv_w_dw[j], conv_w_out[j])
            ms, st_s = conv_mixer_sample(hs, state_conv[j], conv_w_in[j], conv_w_dw[j], conv_w_out[j])
            conv_p.append(st_p)
            conv_s.append(st_s)
        else:
            mp, k_p, v_p = attn_mixer_prompt(hp, attn_w_qkv[j], attn_w_o[j], attn_rel_bias[j])
            ms, k_s, v_s = attn_mixer_sample(hs, cache_k[j], cache_v[j], attn_w_qkv[j], attn_w_o[j], attn_rel_bias[j])
            kp_l.append(k_p)
            vp_l.append(v_p)
            ks_l.append(k_s)
            vs_l.append(v_s)
        xp = xp + mp
        xs = xs + ms
        xp = xp + 0.5 * swiglu(rmsnorm(xp, ffn2_norm[l]), ffn2_w_gate[l], ffn2_w_up[l], ffn2_w_down[l])
        xs = xs + 0.5 * swiglu(rmsnorm(xs, ffn2_norm[l]), ffn2_w_gate[l], ffn2_w_up[l], ffn2_w_down[l])
    y_prompt = rmsnorm(xp, final_norm)
    y_sample = rmsnorm(xs, final_norm)
    new_conv_prompt = jnp.stack(conv_p)
    new_conv_sample = jnp.stack(conv_s)
    new_k_prompt = jnp.stack(kp_l)
    new_v_prompt = jnp.stack(vp_l)
    new_k_sample = jnp.stack(ks_l)
    new_v_sample = jnp.stack(vs_l)
    return (y_prompt, y_sample, new_conv_prompt, new_conv_sample, new_k_prompt, new_v_prompt, new_k_sample, new_v_sample)


_drawn_inputs = setup_inputs


def setup_inputs(seed=0):
    import zlib

    import numpy as np

    out = dict(_drawn_inputs(seed))
    spreads = {}
    factors = {'ffn1_norm': 7.869,
     'mix_norm': 9.441,
     'ffn2_norm': 195.49,
     'final_norm': 200.0,
     'state_conv': 20.693,
     'cache_k': 64.0,
     'cache_v': 64.0,
     'attn_rel_bias': 59.616,
     'attn_w_o': 6.408}
    for name, (base, spread) in spreads.items():
        noise = np.random.default_rng([zlib.crc32(name.encode()), seed]).standard_normal(out[name].shape)
        drawn = base * np.exp(spread * noise) if base else spread * noise
        out[name] = __import__('jax').numpy.asarray(drawn.astype(out[name].dtype))
    for name, factor in factors.items():
        out[name] = (out[name] * factor).astype(out[name].dtype)
    return out
```

```python
from contextlib import ExitStack

import numpy as np

import concourse.bass as bass
from concourse import mybir

F32 = mybir.dt.float32
F32R = mybir.dt.float32r
ALU = mybir.AluOpType
ACT = mybir.ActivationFunctionType

P = 128
D_MODEL = 1024
D_FF = 2816
SEQ = 512
DEC_SEQ = 64
PAST = 128
TOK = SEQ + DEC_SEQ
HALF = TOK // 2
DT = D_MODEL // P
FT = D_FF // P
FFN_CHUNKS = (8, 8, 6)
N_FFN = 4
N_NORM = 7
EPS = 1e-6
CHUNK = 64
HEADS = 16
HEAD_DIM = 64
REL_CLIP = 128
QT = SEQ // P
BIAS_W = 512
EXT = 640
MASKED = -1e30
CONV_PAD = 2
UE = CONV_PAD + SEQ + CONV_PAD + DEC_SEQ
W_SLOTS = 4
RAW_SLOTS = 2
AHEAD = 3
UNITS = 2 * (QT + 1)
assert sum(FFN_CHUNKS) == FT


class At:

    def __init__(self, first, step=0, i=0):
        self.first, self.step, self.i = first, step, i

    def of(self, times=1, plus=0):
        c = times * self.first + plus
        if isinstance(self.i, int):
            return c + times * self.step * self.i
        return self.i * (times * self.step) + c

    def half(self):
        assert self.step % 2 == 0
        return At(self.first // 2, self.step // 2, self.i)

    def plus(self, n):
        return At(self.first + n, self.step, self.i)


class Phase:

    def __init__(self, kind, tiles, k, **more):
        self.kind, self.tiles, self.k = kind, tiles, k
        self.rot = 3 if kind in ("conv_in", "qkv") else W_SLOTS
        self.ffn = more.get("ffn", 0)
        self.chunk = more.get("chunk", 0)
        self.norm = more.get("norm")
        self.feeds = more.get("feeds")


def plan():
    phases = []

    def ffn(f, norm):
        for c, n in enumerate(FFN_CHUNKS):
            phases.append(Phase("up", 2 * n, DT, ffn=f, chunk=c, norm=norm if c == 0 else None))
            last = c == len(FFN_CHUNKS) - 1
            phases.append(Phase("down", DT, n, ffn=f, chunk=c, feeds=norm + 1 if last else None))

    ffn(0, 0)
    phases.append(Phase("conv_in", 3 * DT, DT, norm=1))
    phases.append(Phase("conv_out", DT, DT, feeds=2))
    ffn(1, 2)
    ffn(2, 3)
    phases.append(Phase("qkv", 3 * DT, DT, norm=4))
    phases.append(Phase("attn_out", DT, DT, feeds=5))
    ffn(3, 5)
    g = operands = pairs = hidden = made = 0
    rows = {8: 0, 6: 0}
    operands = DT
    x_first = 0
    for n, p in enumerate(phases):
        p.before = phases[n - 1] if n else None
        p.after = phases[n + 1] if n + 1 < len(phases) else None
        p.g = g
        g += p.tiles
        p.row = rows[p.k]
        rows[p.k] += p.tiles
        p.pairs = pairs
        p.hidden = hidden
        p.made = made
        if p.kind in ("up", "conv_in", "qkv"):
            p.needs = x_first
            p.makes = operands
            n_made = p.tiles // 2 if p.kind == "up" else DT
            if p.kind == "up":
                pairs += n_made
            hidden += n_made
            made += n_made if p.kind != "qkv" else 0
            operands += n_made
        else:
            p.needs = phases[n - 1].makes
            p.makes = operands
            if p.feeds is not None and p.feeds < N_NORM - 1:
                x_first = operands
                operands += DT
    return phases, g, rows


PHASES, N_TILES, ROWS = plan()


def user_before(p, tile):
    if p.rot == 3:
        return 3 if tile >= 3 else W_SLOTS
    return 3 if tile < 3 and p.before is not None and p.before.rot == 3 else W_SLOTS


def streaming_conv_chunkattn_macaron(nc, x_t, w8, w6, gains, conv_taps, conv_state, cache_kt, cache_v,
                                     bias_ext, ident_in, y_t, conv_out_state, k_t, v_t):
    with ExitStack() as ctx:
        def sb(name, shape, dt=F32):
            return ctx.enter_context(nc.sbuf_tensor(name, shape, dt))

        def sem(name):
            return ctx.enter_context(nc.semaphore(name))

        x = sb("x", [P, DT, TOK])
        xg_hi = sb("xg_hi", [P, DT, TOK], F32R)
        xg_lo = sb("xg_lo", [P, DT, TOK], F32R)
        hid_hi = sb("hid_hi", [P, DT, TOK], F32R)
        hid_lo = sb("hid_lo", [P, DT, TOK], F32R)
        w_raw = sb("w_raw", [P, RAW_SLOTS, DT * P])
        w_hi = sb("w_hi", [P, W_SLOTS, DT * P], F32R)
        w_lo = sb("w_lo", [P, W_SLOTS, DT * P], F32R)
        rstd = sb("rstd", [P, TOK])
        sumsq = sb("sumsq", [P, TOK])
        sq = sb("sq", [P, 2, TOK])
        scaled = sb("scaled", [P, TOK])
        scaled2 = sb("scaled2", [P, TOK])
        silu = sb("silu", [P, TOK])
        hidden = sb("hidden", [P, TOK])
        gain = sb("gain", [P, N_NORM, DT])
        taps = sb("taps", [P, 3, DT])
        eps = sb("eps", [P, 1])
        ones = sb("ones", [P, P])
        ident = sb("ident", [P, P])
        state_in = sb("state_in", [P, DT, CONV_PAD])
        state_out = sb("state_out", [P, DT, 2 * CONV_PAD])
        ue = sb("ue", [P, 2, UE])
        conv_y = sb("conv_y", [P, UE - CONV_PAD])
        q_t = sb("q_t", [P, 2, TOK])
        k_sb = sb("k_sb", [P, 2, TOK])
        v_sb = sb("v_sb", [P, 2, TOK])
        v_tok = sb("v_tok", [P, QT + 1, P])
        kc = sb("kc", [P, 2, PAST])
        vc = sb("vc", [P, 2, P])
        bias = sb("bias", [P, 2, BIAS_W])
        scores = sb("scores", [P, 2, BIAS_W])
        probs = sb("probs", [P, 2, BIAS_W])
        probs_t = sb("probs_t", [P, 2, BIAS_W])
        row_max = sb("row_max", [P, UNITS])
        neg_max = sb("neg_max", [P, UNITS])
        row_sum = sb("row_sum", [P, UNITS])
        inv_sum = sb("inv_sum", [P, UNITS])
        ps = ctx.enter_context(nc.psum_tensor("ps", [P, 8, 512], F32))

        x_loaded = [sem(f"x_loaded{m}") for m in range(DT)]
        gain_loaded = sem("gain_loaded")
        consts_loaded = sem("consts_loaded")
        raw_loaded = [sem(f"raw_loaded{s}") for s in range(RAW_SLOTS)]
        w_hi_done = sem("w_hi_done")
        w_split = sem("w_split")
        tile_done = sem("tile_done")
        tile_read = sem("tile_read")
        setup_done = sem("setup_done")
        operand_ready = sem("operand_ready")
        xg_hi_done = sem("xg_hi_done")
        sq_done = sem("sq_done")
        sq_added = sem("sq_added")
        sumsq_done = sem("sumsq_done")
        rms_done = sem("rms_done")
        rstd_done = sem("rstd_done")
        silu_done = sem("silu_done")
        hidden_made = sem("hidden_made")
        hidden_hi_done = sem("hidden_hi_done")
        u_made = sem("u_made")
        state_set = sem("state_set")
        tap0_done = sem("tap0_done")
        taps_done = sem("taps_done")
        state_kept = sem("state_kept")
        kv_stored = [sem(f"kv_stored{s}") for s in range(2)]
        bias_loaded = [sem(f"bias_loaded{s}") for s in range(2)]
        cache_loaded = [sem(f"cache_loaded{s}") for s in range(2)]
        scores_done = sem("scores_done")
        scores_read = sem("scores_read")
        neg_max_done = sem("neg_max_done")
        exp_done = sem("exp_done")
        inv_sum_done = sem("inv_sum_done")
        probs_ready = sem("probs_ready")
        turned = sem("turned")
        turned_read = sem("turned_read")
        pv_done = sem("pv_done")
        y_made = sem("y_made")
        stored = sem("stored")
        state_stored = sem("state_stored")

        def banks(slot):
            return ps[:, 2 * slot:2 * slot + 2, 0:HALF]

        def halves(ap):
            return ap.rearrange("p (b c) -> p b c", b=2)

        SUM_SLOT = 3
        S_BANK, T_BANK, O_BANK, OS_BANK = 2, 4, 6, 7

        def ahead(p, at, tile):
            t = tile + AHEAD
            if t < p.tiles:
                return p, at.plus(AHEAD), t % p.rot, user_before(p, t)
            n = p.after
            if n is None:
                return None
            t -= p.tiles
            return n, At(n.g + t), t % n.rot, user_before(n, t)

        def unit_of(u):
            e, i = divmod(u, QT + 1)
            return e, i, PAST + DEC_SEQ if i == QT else P * (i + 1)

        LAST_SLOT = UNITS + 3
        SLOT_AT = {(n * (3 * DT - 2)) // (LAST_SLOT - 1): n for n in range(LAST_SLOT)}
        assert len(SLOT_AT) == LAST_SLOT

        block = ctx.enter_context(nc.Block())

        @block.sync
        def _(sp):
            sp.sem_inc(w_split, RAW_SLOTS)
            sp.sem_inc(tile_done, W_SLOTS)
            sp.sem_inc(tile_read, W_SLOTS)
            sp.sem_inc(sq_added, 2)
            sp.sem_inc(scores_read, 2)
            sp.sem_inc(turned_read, 2)
            sp.sem_inc(pv_done, 2)
            for s in range(2):
                sp.sem_inc(kv_stored[s], 32)
            for m in range(DT):
                sp.dma_start(x[:, m, :], x_t[m]).then_inc(x_loaded[m], 16)
                if m == 0:
                    sp.dma_start(gain[:, :, :], gains).then_inc(gain_loaded, 16)
            for p in PHASES:
                stream = w8 if p.k == 8 else w6
                with sp.Fori(0, p.tiles // RAW_SLOTS) as i:
                    for s in range(RAW_SLOTS):
                        at = At(p.g + s, RAW_SLOTS, i)
                        sp.wait_ge(w_split, at.of(1, 1))
                        row = At(p.row + s, RAW_SLOTS, i).of()
                        sp.dma_start(w_raw[:, s, 0:p.k * P], stream[bass.ds(row, 1)].rearrange("a p n -> p (a n)")
                                     ).then_inc(raw_loaded[s], 16)
            for m in range(DT):
                sp.wait_ge(y_made, m + 1)
                sp.dma_start(y_t[m], x[:, m, :]).then_inc(stored, 16)
            sp.wait_ge(stored, 16 * DT)
            sp.wait_ge(state_stored, 16)
            for s in range(2):
                sp.wait_ge(kv_stored[s], 32 + 32 * (DT // 2))

        @block.gpsimd
        def _(pool):
            pool.memset(ones[:, :], 1.0)
            pool.memset(eps[:, :], EPS)
            pool.memset(ue[:, :, 0:CONV_PAD], 0.0)
            pool.memset(bias[0:CHUNK, :, 0:CHUNK], MASKED).then_inc(setup_done, 1)
            pool.dma_start(taps[:, :, :], conv_taps).then_inc(consts_loaded, 16)
            pool.dma_start(state_in[:, :, :], conv_state).then_inc(consts_loaded, 16)
            pool.dma_start(ident[:, :], ident_in).then_inc(consts_loaded, 16)

            def sum_squares(n):
                for m in range(DT):
                    pool.wait_ge(sq_done, DT * n + m + 1)
                    if m == 0:
                        if n:
                            pool.wait_ge(sumsq_done, n)
                        ins = pool.tensor_copy(sumsq[:, :], sq[:, 0, :])
                    else:
                        pool.wait_ge(sq_added, 2 + DT * n + m)
                        ins = pool.tensor_tensor(sumsq[:, :], sumsq[:, :], sq[:, m % 2, :], ALU.add)
                    ins.then_inc(sq_added, 1)

            def load_bias(t, e):
                h = 2 * t + e
                row = bias_ext[h]
                for first, end, left in ((0, CHUNK, CHUNK), (CHUNK, P, 0)):
                    src = bass.AP(tensor=row.tensor, offset=row.offset + first + left,
                                  ap=[[1, end - first], [1, BIAS_W - left]])
                    pool.dma_start(bias[first:end, e, left:BIAS_W], src).then_inc(bias_loaded[e], 16)

            def load_cache(t):
                pool.dma_start(kc[:, t % 2, :], cache_kt[t]).then_inc(cache_loaded[t % 2], 16)
                pool.dma_start(vc[:, t % 2, :], cache_v[t]).then_inc(cache_loaded[t % 2], 16)

            pool.wait_ge(setup_done, 1)
            for e in range(2):
                load_bias(0, e)
            for t in range(2):
                load_cache(t)
            for p in PHASES:
                if p.norm is not None:
                    sum_squares(p.norm)
                if p.kind == "conv_out":
                    pool.wait_ge(state_kept, DT)
                    pool.dma_start(conv_out_state, state_out[:, :, :]).then_inc(state_stored, 16)
                if p.kind == "qkv":
                    for t in range(DT):
                        if t >= 1:
                            for e in range(2):
                                pool.wait_ge(scores_read, 2 + UNITS * (t - 1) + (QT + 1) * (e + 1))
                                load_bias(t, e)
                            if t >= 2:
                                pool.wait_ge(pv_done, 2 + UNITS * (t - 1))
                                load_cache(t)
            sum_squares(N_NORM - 1)

        @block.scalar
        def _(act):
            def split_hi(nxt):
                if nxt is None:
                    return
                p, at, slot, back = nxt
                raw = (p.g + at.first - p.g) % RAW_SLOTS
                act.wait_ge(raw_loaded[raw], at.half().of(16, 16))
                act.wait_ge(tile_done, at.of(1, W_SLOTS - back + 1))
                act.activation(w_hi[:, slot, 0:p.k * P], w_raw[:, raw, 0:p.k * P], ACT.Copy).then_inc(w_hi_done, 1)

            def norm_input(n, m, last):
                if not last:
                    act.activation(xg_hi[:, m, :], x[:, m, :], ACT.Copy, scale=gain[:, n, m:m + 1]).then_inc(xg_hi_done, 1)
                act.wait_ge(sq_added, DT * n + m + 1)
                act.activation(sq[:, m % 2, :], x[:, m, :], ACT.Square).then_inc(sq_done, 1)

            def root(n):
                act.wait_ge(sumsq_done, n + 1)
                if n == 0:
                    act.wait_ge(setup_done, 1)
                act.activation(halves(rstd[:, :]), banks(SUM_SLOT), ACT.Sqrt,
                               bias=eps[:, :], scale=1.0 / D_MODEL).then_inc(rms_done, 1)

            def split_hidden(tile, made):
                act.wait_ge(hidden_made, made.of(1, 1))
                act.activation(hid_hi[:, bass.ds(tile, 1), :].rearrange("p a n -> p (a n)"), hidden[:, :],
                               ACT.Copy).then_inc(hidden_hi_done, 1)

            def attend(slot, t):
                if slot == 0:
                    for n, (bank, out) in enumerate(((T_BANK + 1, v_tok[:, 0:QT, :].rearrange("p a n -> p (a n)")),
                                                     (T_BANK, v_tok[0:DEC_SEQ, QT, :]))):
                        act.wait_ge(turned, t.of(UNITS + 2, n + 1))
                        rows = P if n == 0 else DEC_SEQ
                        act.activation(out, ps[0:rows, bank, 0:out.shape[1]], ACT.Copy).then_inc(turned_read, 1)
                u = slot - 2
                if 0 <= u < UNITS:
                    e, i, width = unit_of(u)
                    act.wait_ge(turned, t.of(UNITS + 2, u + 3))
                    act.wait_ge(pv_done, t.of(UNITS, u + 1))
                    if i < QT:
                        act.activation(probs_t[:, u % 2, 0:width], ps[:, T_BANK + u % 2, 0:width],
                                       ACT.Copy).then_inc(turned_read, 1)
                    else:
                        act.activation(probs_t[:, u % 2, 0:P], ps[:, T_BANK + u % 2, 0:P], ACT.Copy)
                        act.activation(probs_t[0:DEC_SEQ, u % 2, P:2 * P], ps[0:DEC_SEQ, T_BANK + u % 2, P:2 * P],
                                       ACT.Copy).then_inc(turned_read, 1)
                u = slot
                if u < UNITS:
                    e, i, width = unit_of(u)
                    act.wait_ge(neg_max_done, t.of(UNITS, u + 1))
                    act.activation(probs[:, u % 2, 0:width], scores[:, u % 2, 0:width], ACT.Exp,
                                   bias=neg_max[:, u:u + 1], scale=1.0,
                                   accum_out=row_sum[:, u:u + 1]).then_inc(exp_done, 1)

            def attended(t):
                act.wait_ge(pv_done, t.of(UNITS, 2 + UNITS))
                tile = bass.ds(t.of(), 1)
                act.activation(hid_hi[:, tile, 0:SEQ].rearrange("p a n -> p (a n)"), ps[:, O_BANK, :], ACT.Copy)
                act.activation(hid_hi[:, tile, SEQ:TOK].rearrange("p a n -> p (a n)"), ps[:, OS_BANK, 0:DEC_SEQ],
                               ACT.Copy).then_inc(hidden_hi_done, 1)

            act.wait_ge(gain_loaded, 16)
            for m in range(DT):
                act.wait_ge(x_loaded[m], 16)
                norm_input(0, m, False)
            for t in range(AHEAD):
                split_hi((PHASES[0], At(t), t, W_SLOTS))

            def up(p, i, tiles):
                for u in tiles:
                    at = At(p.g + u, 4, i)
                    split_hi(ahead(p, at, u + 4 * i if isinstance(i, int) else u))
                    if p.norm is not None and isinstance(i, int) and i == 0 and u == 0:
                        root(p.norm)
                    if u % 2 == 0:
                        act.wait_ge(tile_read, at.of(1, W_SLOTS + 1))
                        act.activation(silu[:, :], scaled[:, :], ACT.Silu).then_inc(silu_done, 1)
                    else:
                        split_hidden(At(u // 2, 2, i).of(), At(p.made + u // 2, 2, i))

            def down(p):
                for m in range(DT):
                    at = At(p.g + m)
                    split_hi(ahead(p, at, m))
                    if p.feeds is not None:
                        act.wait_ge(tile_read, at.of(1, W_SLOTS + 1))
                        norm_input(p.feeds, m, p.feeds == N_NORM - 1)

            def conv(p, i, js):
                if isinstance(i, int) and i == 0:
                    act.wait_ge(consts_loaded, 48)
                for jj in js:
                    j = At(jj, 2, i)
                    slot = jj % 2
                    for r in range(3):
                        at = At(p.g + 3 * jj + r, 6, i)
                        split_hi(ahead(p, at, 3 * jj + r + (6 * i if isinstance(i, int) else 0)))
                        if r == 0:
                            if p.norm is not None and isinstance(i, int) and i == 0 and jj == 0:
                                root(p.norm)
                            act.activation(ue[:, slot, CONV_PAD + SEQ:2 * CONV_PAD + SEQ],
                                           state_in[:, bass.ds(j.of(), 1), :].rearrange("p a n -> p (a n)"),
                                           ACT.Copy).then_inc(state_set, 1)
                        if r == 1:
                            act.wait_ge(u_made, j.of(1, 1))
                            act.wait_ge(state_set, j.of(1, 1))
                            act.activation(conv_y[:, :], ue[:, slot, 0:UE - CONV_PAD], ACT.Copy,
                                           scale=taps[:, 0, bass.ds(j.of(), 1)]).then_inc(tap0_done, 1)
                            so = state_out[:, bass.ds(j.of(), 1), :].rearrange("p a n -> p (a n)")
                            act.activation(so[:, 0:CONV_PAD], ue[:, slot, SEQ:SEQ + CONV_PAD], ACT.Copy)
                            act.activation(so[:, CONV_PAD:2 * CONV_PAD], ue[:, slot, UE - CONV_PAD:UE],
                                           ACT.Copy).then_inc(state_kept, 1)
                        if r == 2:
                            split_hidden(j.of(), At(p.made + jj, 2, i))

            def qkv(p, t, with_attention):
                before = t.plus(-1)
                for r in range(3):
                    for k in range(DT):
                        slot = SLOT_AT.get(DT * r + k - 1) if with_attention else None
                        if k == 0 and r > 0:
                            finish_tile(p, t, r - 1)
                        if slot is not None:
                            attend(slot, before)
                finish_tile(p, t, 2)
                if with_attention:
                    attended(before)

            def finish_tile(p, t, r):
                local = 3 * t.first + r
                at = At(p.g + local, 3 * t.step, t.i)
                if not isinstance(t.i, int):
                    split_hi(ahead(p, at, local))
                else:
                    split_hi(ahead(p, At(p.g + 3 * t.of() + r), 3 * t.of() + r))
                if isinstance(t.i, int) and t.of() == 0 and r == 0:
                    root(p.norm)
                if r == 2:
                    act.wait_ge(tile_read, at.of(1, W_SLOTS + 1))
                    odd = t.first % 2 if not isinstance(t.i, int) else t.of() % 2
                    for src, dst in ((k_sb, k_t), (v_sb, v_t)):
                        act.dma_start(dst[bass.ds(t.of(), 1)].rearrange("a p n -> p (a n)"), src[:, odd, :]
                                      ).then_inc(kv_stored[odd], 16)

            for p in PHASES:
                if p.kind == "up":
                    n = p.tiles // 4
                    up(p, 0, range(4))
                    if n > 2:
                        with act.Fori(1, n - 1) as i:
                            up(p, i, range(4))
                    up(p, n - 1, range(4))
                elif p.kind == "conv_in":
                    n = p.tiles // 6
                    conv(p, 0, range(2))
                    with act.Fori(1, n - 1) as i:
                        conv(p, i, range(2))
                    conv(p, n - 1, range(2))
                elif p.kind == "qkv":
                    qkv(p, At(0), False)
                    with act.Fori(0, (DT - 2) // 2) as i:
                        qkv(p, At(1, 2, i), True)
                        qkv(p, At(2, 2, i), True)
                    qkv(p, At(DT - 1), True)
                    for slot in range(LAST_SLOT):
                        attend(slot, At(DT - 1))
                    attended(At(DT - 1))
                else:
                    down(p)
            root(N_NORM - 1)

        @block.vector
        def _(dve):
            def split_lo(nxt):
                if nxt is None:
                    return
                p, at, slot, back = nxt
                raw = at.first % RAW_SLOTS
                dve.wait_ge(w_hi_done, at.of(1, 1))
                dve.tensor_tensor(w_lo[:, slot, 0:p.k * P], w_raw[:, raw, 0:p.k * P],
                                  w_hi[:, slot, 0:p.k * P].bitcast(F32), ALU.subtract).then_inc(w_split, 1)

            def norm_lo(n, m):
                dve.wait_ge(xg_hi_done, DT * n + m + 1)
                dve.scalar_tensor_tensor(xg_lo[:, m, :], x[:, m, :], gain[:, n, m:m + 1], xg_hi[:, m, :].bitcast(F32),
                                         ALU.mult, ALU.subtract).then_inc(operand_ready, 1)

            def invert(n):
                dve.wait_ge(rms_done, n + 1)
                dve.reciprocal(rstd[:, :], rstd[:, :]).then_inc(rstd_done, 1)
                dve.wait_ge(rstd_done, n + 1)

            def split_hidden(tile, made):
                dve.wait_ge(hidden_hi_done, made.of(1, 1))
                dve.tensor_tensor(hid_lo[:, bass.ds(tile, 1), :].rearrange("p a n -> p (a n)"), hidden[:, :],
                                  hid_hi[:, bass.ds(tile, 1), :].rearrange("p a n -> p (a n)").bitcast(F32),
                                  ALU.subtract).then_inc(operand_ready, 1)

            def attend(slot, t):
                u = slot
                if u < UNITS:
                    e, i, width = unit_of(u)
                    if u % (QT + 1) == 0:
                        dve.wait_ge(bias_loaded[e], t.of(32, 32))
                    dve.wait_ge(scores_done, t.of(UNITS, u + 1))
                    dve.tensor_tensor(scores[:, u % 2, 0:width], ps[:, S_BANK + u % 2, 0:width],
                                      bias[:, e, 0:width][:, ::-1], ALU.add).then_inc(scores_read, 1)
                    dve.wait_ge(scores_read, t.of(UNITS, 2 + u + 1))
                    dve.tensor_reduce(neg_max[:, u:u + 1], scores[:, u % 2, 0:width],
                                      mybir.AxisListType.X, ALU.max, negate=True).then_inc(neg_max_done, 1)
                u = slot - 1
                if 0 <= u < UNITS:
                    e, i, width = unit_of(u)
                    dve.wait_ge(exp_done, t.of(UNITS, u + 1))
                    dve.reciprocal(inv_sum[:, u:u + 1], row_sum[:, u:u + 1]).then_inc(inv_sum_done, 1)
                    dve.wait_ge(inv_sum_done, t.of(UNITS, u + 1))
                    dve.tensor_scalar(probs[:, u % 2, 0:width], probs[:, u % 2, 0:width],
                                      inv_sum[:, u:u + 1], None, ALU.mult).then_inc(probs_ready, 1)

            def attended(p, t):
                tile = bass.ds(t.of(), 1)
                dve.wait_ge(hidden_hi_done, t.of(1, p.hidden + 1))
                dve.tensor_tensor(hid_lo[:, tile, 0:SEQ].rearrange("p a n -> p (a n)"), ps[:, O_BANK, :],
                                  hid_hi[:, tile, 0:SEQ].rearrange("p a n -> p (a n)").bitcast(F32), ALU.subtract)
                dve.tensor_tensor(hid_lo[:, tile, SEQ:TOK].rearrange("p a n -> p (a n)"), ps[:, OS_BANK, 0:DEC_SEQ],
                                  hid_hi[:, tile, SEQ:TOK].rearrange("p a n -> p (a n)").bitcast(F32),
                                  ALU.subtract).then_inc(operand_ready, 1)

            dve.wait_ge(gain_loaded, 16)
            for m in range(DT):
                norm_lo(0, m)
            for t in range(AHEAD):
                split_lo((PHASES[0], At(t), t, W_SLOTS))

            def up(p, i, tiles):
                for u in tiles:
                    at = At(p.g + u, 4, i)
                    if p.norm is not None and isinstance(i, int) and i == 0 and u == 0:
                        split_lo(ahead(p, at, 0))
                        invert(p.norm)
                    dve.wait_ge(tile_done, at.of(1, W_SLOTS + 1))
                    out = scaled if u % 2 == 0 else scaled2
                    dve.tensor_tensor(halves(out[:, :]), banks(u), halves(rstd[:, :]), ALU.mult).then_inc(tile_read, 1)
                    if u % 2:
                        dve.wait_ge(silu_done, At(p.pairs + u // 2, 2, i).of(1, 1))
                        dve.wait_ge(tile_read, at.of(1, W_SLOTS + 1))
                        dve.tensor_tensor(hidden[:, :], silu[:, :], scaled2[:, :], ALU.mult).then_inc(hidden_made, 1)
                    if not (p.norm is not None and isinstance(i, int) and i == 0 and u == 0):
                        split_lo(ahead(p, at, u + 4 * i if isinstance(i, int) else u))
                    if u % 2:
                        split_hidden(At(u // 2, 2, i).of(), At(p.hidden + u // 2, 2, i))

            def down(p):
                share = 0.5 if p.kind == "down" else 1.0
                for m in range(DT):
                    at = At(p.g + m)
                    dve.wait_ge(tile_done, at.of(1, W_SLOTS + 1))
                    dve.scalar_tensor_tensor(halves(x[:, m, :]), banks(m % W_SLOTS), share, halves(x[:, m, :]),
                                             ALU.mult, ALU.add).then_inc(tile_read, 1)
                    split_lo(ahead(p, at, m))
                    if p.feeds is not None and p.feeds < N_NORM - 1:
                        norm_lo(p.feeds, m)

            def conv(p, i, js):
                for jj in js:
                    j = At(jj, 2, i)
                    slot = jj % 2
                    for r in range(3):
                        at = At(p.g + 3 * jj + r, 6, i)
                        first = isinstance(i, int) and i == 0 and jj == 0 and r == 0
                        if first:
                            dve.wait_ge(consts_loaded, 48)
                            dve.wait_ge(setup_done, 1)
                        nxt = ahead(p, at, 3 * jj + r + (6 * i if isinstance(i, int) else 0))
                        if first:
                            invert(p.norm)
                        dve.wait_ge(tile_done, at.of(1, W_SLOTS + 1))
                        if r == 0:
                            dve.tensor_tensor(halves(scaled[:, :]), banks(r), halves(rstd[:, :]),
                                              ALU.mult).then_inc(tile_read, 1)
                            split_lo(nxt)
                        if r == 1:
                            dve.wait_ge(tile_read, at.of(1, W_SLOTS))
                            dve.tensor_tensor(halves(scaled2[:, :]), banks(r), halves(scaled[:, :]),
                                              ALU.mult).then_inc(tile_read, 1)
                            dve.wait_ge(tile_read, at.of(1, W_SLOTS + 1))
                            dve.tensor_tensor(ue[:, slot, CONV_PAD:CONV_PAD + SEQ], scaled2[:, 0:SEQ],
                                              rstd[:, 0:SEQ], ALU.mult)
                            dve.tensor_tensor(ue[:, slot, 2 * CONV_PAD + SEQ:UE], scaled2[:, SEQ:TOK],
                                              rstd[:, SEQ:TOK], ALU.mult).then_inc(u_made, 1)
                            split_lo(nxt)
                            dve.wait_ge(tap0_done, j.of(1, 1))
                            for k in range(1, 3):
                                if k == 2:
                                    dve.wait_ge(taps_done, j.of(2, 1))
                                dve.scalar_tensor_tensor(conv_y[:, :], ue[:, slot, k:k + UE - CONV_PAD],
                                                         taps[:, k, bass.ds(j.of(), 1)], conv_y[:, :],
                                                         ALU.mult, ALU.add).then_inc(taps_done, 1)
                        if r == 2:
                            dve.tensor_tensor(halves(silu[:, :]), banks(r), halves(rstd[:, :]),
                                              ALU.mult).then_inc(tile_read, 1)
                            dve.wait_ge(tile_read, at.of(1, W_SLOTS + 1))
                            dve.wait_ge(taps_done, j.of(2, 2))
                            dve.tensor_tensor(hidden[:, 0:SEQ], silu[:, 0:SEQ], conv_y[:, 0:SEQ], ALU.mult)
                            dve.tensor_tensor(hidden[:, SEQ:TOK], silu[:, SEQ:TOK],
                                              conv_y[:, SEQ + CONV_PAD:UE - CONV_PAD], ALU.mult
                                              ).then_inc(hidden_made, 1)
                            split_lo(nxt)
                            split_hidden(j.of(), At(p.hidden + jj, 2, i))

            def qkv(p, t, with_attention):
                before = t.plus(-1)
                for r in range(3):
                    for k in range(DT):
                        slot = SLOT_AT.get(DT * r + k - 1) if with_attention else None
                        if k == 0 and r > 0:
                            finish_tile(p, t, r - 1)
                        if slot is not None:
                            attend(slot, before)
                finish_tile(p, t, 2)
                if with_attention:
                    attended(p, before)

            def finish_tile(p, t, r):
                if isinstance(t.i, int):
                    local = 3 * t.of() + r
                    at = At(p.g + local)
                    odd = t.of() % 2
                else:
                    local = 3 * t.first + r
                    at = At(p.g + local, 3 * t.step, t.i)
                    odd = t.first % 2
                if isinstance(t.i, int) and t.of() == 0 and r == 0:
                    invert(p.norm)
                dve.wait_ge(tile_done, at.of(1, W_SLOTS + 1))
                if r == 1:
                    dve.wait_ge(kv_stored[odd], t.half().of(32, 32))
                out = (q_t, k_sb, v_sb)[r]
                dve.scalar_tensor_tensor(halves(out[:, odd, :]), banks(0), HEAD_DIM ** -0.5 if r == 0 else 1.0,
                                         halves(rstd[:, :]), ALU.mult, ALU.mult).then_inc(tile_read, 1)
                split_lo(ahead(p, at, local))

            for p in PHASES:
                if p.kind == "up":
                    n = p.tiles // 4
                    up(p, 0, range(4))
                    if n > 2:
                        with dve.Fori(1, n - 1) as i:
                            up(p, i, range(4))
                    up(p, n - 1, range(4))
                elif p.kind == "conv_in":
                    n = p.tiles // 6
                    conv(p, 0, range(2))
                    with dve.Fori(1, n - 1) as i:
                        conv(p, i, range(2))
                    conv(p, n - 1, range(2))
                elif p.kind == "qkv":
                    qkv(p, At(0), False)
                    with dve.Fori(0, (DT - 2) // 2) as i:
                        qkv(p, At(1, 2, i), True)
                        qkv(p, At(2, 2, i), True)
                    qkv(p, At(DT - 1), True)
                    for slot in range(LAST_SLOT):
                        attend(slot, At(DT - 1))
                    attended(p, At(DT - 1))
                else:
                    down(p)
            invert(N_NORM - 1)
            for m in range(DT):
                dve.scalar_tensor_tensor(x[:, m, :], x[:, m, :], gain[:, N_NORM - 1, m:m + 1], rstd[:, :],
                                         ALU.mult, ALU.mult).then_inc(y_made, 1)

        @block.tensor
        def _(pe):
            def product(p, at, w_slot, out_slot, back, operand, wait_operand, between=None):
                hi, lo = operand
                pe.wait_ge(w_split, at.of(1, RAW_SLOTS + 1))
                pe.wait_ge(tile_read, at.of(1, W_SLOTS - back + 1))
                for k in range(p.k):
                    if wait_operand:
                        pe.wait_ge(operand_ready, p.needs + k + 1)
                    w = slice(k * P, (k + 1) * P)
                    for n, (wt, xt) in enumerate(((w_hi, hi), (w_hi, lo), (w_lo, hi))):
                        for b in range(2):
                            mm = pe.matmul(ps[:, 2 * out_slot + b, 0:HALF], wt[:, w_slot, w],
                                           xt[:, k, b * HALF:(b + 1) * HALF],
                                           start=(k == 0 and n == 0), stop=(k == p.k - 1 and n == 2))
                    if k == p.k - 1:
                        mm.then_inc(tile_done, 1)
                    elif between is not None:
                        between(k)

            def sum_over_partitions(n):
                if n == 0:
                    pe.wait_ge(setup_done, 1)
                pe.wait_ge(sq_added, 2 + DT * (n + 1))
                for b in range(2):
                    mm = pe.matmul(ps[:, 2 * SUM_SLOT + b, 0:HALF], ones[:, :],
                                   sumsq[:, b * HALF:(b + 1) * HALF], start=True, stop=True)
                mm.then_inc(sumsq_done, 1)

            def attend(slot, t, odd):
                if slot == 0:
                    pe.wait_ge(turned_read, t.of(UNITS + 2, 2))
                    for c in range(QT):
                        mm = pe.transpose(ps[:, T_BANK + 1, c * P:(c + 1) * P], v_sb[:, odd, c * P:(c + 1) * P],
                                          ident[:, :])
                    mm.then_inc(turned, 1)
                    pe.transpose(ps[0:DEC_SEQ, T_BANK, 0:P], v_sb[:, odd, SEQ:TOK], ident[:, :]).then_inc(turned, 1)
                u = slot
                if u < UNITS:
                    e, i, width = unit_of(u)
                    hd = slice(HEAD_DIM * e, HEAD_DIM * (e + 1))
                    pe.wait_ge(scores_read, t.of(UNITS, u + 1))
                    if u == 0:
                        pe.wait_ge(cache_loaded[odd], t.half().of(32, 32))
                    if i < QT:
                        mm = pe.matmul(ps[:, S_BANK + u % 2, 0:width], q_t[hd, odd, i * P:(i + 1) * P],
                                       k_sb[hd, odd, 0:width], start=True, stop=True)
                    else:
                        pe.matmul(ps[:, S_BANK + u % 2, 0:PAST], q_t[hd, odd, TOK - P:TOK], kc[hd, odd, :],
                                  start=True, stop=True)
                        mm = pe.matmul(ps[:, S_BANK + u % 2, PAST:width], q_t[hd, odd, TOK - P:TOK],
                                       k_sb[hd, odd, SEQ:TOK], start=True, stop=True)
                    mm.then_inc(scores_done, 1)
                u = slot - 2
                if 0 <= u < UNITS:
                    e, i, width = unit_of(u)
                    pe.wait_ge(probs_ready, t.of(UNITS, u + 1))
                    pe.wait_ge(turned_read, t.of(UNITS + 2, u + 3))
                    if i < QT:
                        for c in range(i + 1):
                            mm = pe.transpose(ps[:, T_BANK + u % 2, c * P:(c + 1) * P],
                                              probs[:, u % 2, c * P:(c + 1) * P], ident[:, :])
                    else:
                        pe.transpose(ps[:, T_BANK + u % 2, 0:P], probs[:, u % 2, 0:PAST], ident[:, :])
                        mm = pe.transpose(ps[0:DEC_SEQ, T_BANK + u % 2, P:2 * P],
                                          probs[:, u % 2, PAST:width], ident[:, :])
                    mm.then_inc(turned, 1)
                u = slot - 3
                if 0 <= u < UNITS:
                    e, i, width = unit_of(u)
                    hd = slice(HEAD_DIM * e, HEAD_DIM * (e + 1))
                    pe.wait_ge(turned_read, t.of(UNITS + 2, 2 + u + 3))
                    if i < QT:
                        for c in range(i + 1):
                            mm = pe.matmul(ps[hd, O_BANK, i * P:(i + 1) * P], v_tok[:, c, hd],
                                           probs_t[:, u % 2, c * P:(c + 1) * P], start=(c == 0), stop=(c == i))
                    else:
                        pe.matmul(ps[hd, OS_BANK, 0:DEC_SEQ], vc[:, odd, hd], probs_t[:, u % 2, P - DEC_SEQ:P],
                                  start=True, stop=False)
                        mm = pe.matmul(ps[hd, OS_BANK, 0:DEC_SEQ], v_tok[0:DEC_SEQ, QT, hd],
                                       probs_t[0:DEC_SEQ, u % 2, 2 * P - DEC_SEQ:2 * P], start=False, stop=True)
                    mm.then_inc(pv_done, 1)

            def qkv(p, t, with_attention):
                odd = (t.of() if isinstance(t.i, int) else t.first) % 2
                before = t.plus(-1)
                first = isinstance(t.i, int) and t.of() == 0
                for r in range(3):
                    at = At(p.g + 3 * t.first + r, 3 * t.step, t.i)

                    def between(k):
                        slot = SLOT_AT.get(DT * r + k)
                        if slot is not None:
                            if slot == 3 and not (isinstance(before.i, int) and before.of() == 0):
                                pe.wait_ge(operand_ready, before.of(1, p.makes))
                            attend(slot, before, 1 - odd)

                    w_slot = (3 * t.first + r) % 3
                    product(p, at, w_slot, 0, 1, (xg_hi, xg_lo), first and r == 0,
                            between if with_attention else None)
                    if first and r == 0:
                        sum_over_partitions(p.norm)
                    if with_attention:
                        between(DT - 1)

            def tiles(p, operand, i, n, wait_operand):
                for u in range(n):
                    peeled = isinstance(i, int)
                    local = u + n * i if peeled else u
                    back = user_before(p, local) if peeled else p.rot
                    if peeled and local == SUM_SLOT and p.norm is not None:
                        pe.wait_ge(rms_done, p.norm + 1)
                    product(p, At(p.g + u, n, i), u % p.rot, u % p.rot, back, operand, wait_operand and u == 0)
                    if peeled and local == 0 and p.norm is not None:
                        sum_over_partitions(p.norm)

            for p in PHASES:
                if p.kind == "up":
                    tiles(p, (xg_hi, xg_lo), 0, 4, p.norm is not None)
                    with pe.Fori(1, p.tiles // 4) as i:
                        tiles(p, (xg_hi, xg_lo), i, 4, False)
                elif p.kind == "conv_in":
                    tiles(p, (xg_hi, xg_lo), 0, 6, True)
                    with pe.Fori(1, p.tiles // 6) as i:
                        tiles(p, (xg_hi, xg_lo), i, 6, False)
                elif p.kind == "qkv":
                    qkv(p, At(0), False)
                    pe.wait_ge(consts_loaded, 48)
                    with pe.Fori(0, (DT - 2) // 2) as i:
                        qkv(p, At(1, 2, i), True)
                        qkv(p, At(2, 2, i), True)
                    qkv(p, At(DT - 1), True)
                    pe.wait_ge(operand_ready, p.makes + DT - 1)
                    for slot in range(LAST_SLOT):
                        attend(slot, At(DT - 1), (DT - 1) % 2)
                elif p.kind == "down":
                    with pe.Fori(0, p.tiles // 4) as i:
                        tiles(p, (hid_hi, hid_lo), i, 4, True)
                else:
                    for i in range(p.tiles // 4):
                        tiles(p, (hid_hi, hid_lo), i, 4, i == 0)
            sum_over_partitions(N_NORM - 1)


def weight_tiles(w):
    k, m = w.shape[0] // P, w.shape[1] // P
    return w.reshape(k, P, m, P).transpose(2, 1, 0, 3).reshape(m, P, k * P)


def interleaved(*ws):
    return np.stack([weight_tiles(w) for w in ws], axis=1).reshape(-1, P, ws[0].shape[0])


def kernel(x_prompt, x_sample, state_conv, cache_k, cache_v,
           ffn1_norm, ffn1_w_gate, ffn1_w_up, ffn1_w_down,
           mix_norm, conv_w_in, conv_w_dw, conv_w_out,
           attn_w_qkv, attn_w_o, attn_rel_bias,
           ffn2_norm, ffn2_w_gate, ffn2_w_up, ffn2_w_down,
           final_norm):
    import concourse.bacc as _bacc
    from concourse.bass_utils import run_bass_kernel_spmd as _run

    a = {n: np.asarray(v) for n, v in dict(
        x_prompt=x_prompt, x_sample=x_sample, state_conv=state_conv, cache_k=cache_k, cache_v=cache_v,
        ffn1_norm=ffn1_norm, ffn1_w_gate=ffn1_w_gate, ffn1_w_up=ffn1_w_up, ffn1_w_down=ffn1_w_down,
        mix_norm=mix_norm, conv_w_in=conv_w_in, conv_w_dw=conv_w_dw, conv_w_out=conv_w_out,
        attn_w_qkv=attn_w_qkv, attn_w_o=attn_w_o, attn_rel_bias=attn_rel_bias,
        ffn2_norm=ffn2_norm, ffn2_w_gate=ffn2_w_gate, ffn2_w_up=ffn2_w_up, ffn2_w_down=ffn2_w_down,
        final_norm=final_norm).items()}

    streams = {8: [], 6: []}
    for p in PHASES:
        if p.kind in ("up", "down"):
            layer, name = p.ffn // 2, f"ffn{p.ffn % 2 + 1}"
            first = sum(FFN_CHUNKS[:p.chunk]) * P
            part = slice(first, first + FFN_CHUNKS[p.chunk] * P)
            if p.kind == "up":
                w = interleaved(a[name + "_w_gate"][layer][:, part], a[name + "_w_up"][layer][:, part])
            else:
                w = weight_tiles(a[name + "_w_down"][layer][part])
        elif p.kind == "conv_in":
            b, c, h = np.split(a["conv_w_in"][0], 3, axis=1)
            w = interleaved(c, h, b)
        elif p.kind == "qkv":
            w = interleaved(*np.split(a["attn_w_qkv"][0], 3, axis=1))
        else:
            w = weight_tiles(a["conv_w_out" if p.kind == "conv_out" else "attn_w_o"][0])
        streams[p.k].append(w)

    def by_feature(v):
        return np.moveaxis(v.reshape(v.shape[:-1] + (DT, P)), -1, 0)

    tokens = np.concatenate([a["x_prompt"][0], a["x_sample"][0]], axis=0)
    norms = np.stack([a["ffn1_norm"][0], a["mix_norm"][0], a["ffn2_norm"][0],
                      a["ffn1_norm"][1], a["mix_norm"][1], a["ffn2_norm"][1], a["final_norm"]])
    rel = a["attn_rel_bias"][0][:, REL_CLIP - P + 1:]
    rel = np.pad(rel, ((0, 0), (0, EXT - rel.shape[1])), mode="edge")
    ins = {
        "x_t": tokens.T.reshape(DT, P, TOK),
        "w8": np.concatenate(streams[8]),
        "w6": np.concatenate(streams[6]),
        "gains": by_feature(norms),
        "conv_taps": by_feature(a["conv_w_dw"][0]),
        "conv_state": np.moveaxis(by_feature(a["state_conv"][0, 0]), 1, 2),
        "cache_kt": a["cache_k"][0, 0].reshape(PAST, D_MODEL).T.reshape(DT, P, PAST),
        "cache_v": a["cache_v"][0, 0].reshape(PAST, DT, P).transpose(1, 0, 2),
        "bias_ext": rel,
        "ident_in": np.eye(P, dtype=np.float32),
    }
    outs = {
        "y_t": (DT, P, TOK),
        "conv_out_state": (P, DT, 2 * CONV_PAD),
        "k_t": (DT, P, TOK),
        "v_t": (DT, P, TOK),
    }
    nc = _bacc.Bacc("TRN2", target_bir_lowering=False, num_devices=1)
    arrays, args = {}, {}
    for name, v in ins.items():
        arrays[name] = np.ascontiguousarray(v)
        args[name] = nc.dram_tensor(name, arrays[name].shape, F32, kind="ExternalInput").ap()
    for name, shape in outs.items():
        args[name] = nc.dram_tensor(name, shape, F32, kind="ExternalOutput").ap()
    streaming_conv_chunkattn_macaron(nc, **args)
    got = _run(nc, [arrays], core_ids=[0]).results[0]

    y = got["y_t"].reshape(D_MODEL, TOK).T
    k = got["k_t"].reshape(D_MODEL, TOK).T.reshape(TOK, HEADS, HEAD_DIM)
    v = got["v_t"].reshape(D_MODEL, TOK).T.reshape(TOK, HEADS, HEAD_DIM)
    state = got["conv_out_state"].transpose(2, 1, 0).reshape(2, CONV_PAD, D_MODEL)
    c = np.ascontiguousarray
    return (c(y[None, :SEQ]), c(y[None, SEQ:]), c(state[None, 0:1]), c(state[None, 1:2]),
            c(k[None, None, :SEQ]), c(v[None, None, :SEQ]), c(k[None, None, SEQ:]), c(v[None, None, SEQ:]))
```

```python
from contextlib import ExitStack

import numpy as np

import concourse.bass as bass
from concourse import mybir

F32 = mybir.dt.float32
F32R = mybir.dt.float32r
ALU = mybir.AluOpType
ACT = mybir.ActivationFunctionType

P = 128
D_MODEL = 1024
D_FF = 2816
SEQ = 512
DEC_SEQ = 64
PAST = 128
TOK = SEQ + DEC_SEQ
HALF = TOK // 2
DT = D_MODEL // P
FT = D_FF // P
FFN_CHUNKS = (8, 8, 6)
N_FFN = 4
N_NORM = 7
EPS = 1e-6
CHUNK = 64
HEADS = 16
HEAD_DIM = 64
REL_CLIP = 128
QT = SEQ // P
BIAS_W = 512
EXT = 640
MASKED = -1e30
CONV_PAD = 2
UE = CONV_PAD + SEQ + CONV_PAD + DEC_SEQ
W_SLOTS = 4
RAW_SLOTS = 2
AHEAD = 3
PROB_SLOTS = 4
UNITS = 2 * (QT + 1)
assert sum(FFN_CHUNKS) == FT


class At:

    def __init__(self, first, step=0, i=0):
        self.first, self.step, self.i = first, step, i

    def of(self, times=1, plus=0):
        c = times * self.first + plus
        if isinstance(self.i, int):
            return c + times * self.step * self.i
        return self.i * (times * self.step) + c

    def half(self):
        assert self.step % 2 == 0
        return At(self.first // 2, self.step // 2, self.i)

    def plus(self, n):
        return At(self.first + n, self.step, self.i)


class Phase:

    def __init__(self, kind, tiles, k, **more):
        self.kind, self.tiles, self.k = kind, tiles, k
        self.rot = 3 if kind in ("conv_in", "qkv") else W_SLOTS
        self.ffn = more.get("ffn", 0)
        self.chunk = more.get("chunk", 0)
        self.norm = more.get("norm")
        self.feeds = more.get("feeds")


def plan():
    phases = []

    def ffn(f, norm):
        for c, n in enumerate(FFN_CHUNKS):
            phases.append(Phase("up", 2 * n, DT, ffn=f, chunk=c, norm=norm if c == 0 else None))
            last = c == len(FFN_CHUNKS) - 1
            phases.append(Phase("down", DT, n, ffn=f, chunk=c, feeds=norm + 1 if last else None))

    ffn(0, 0)
    phases.append(Phase("conv_in", 3 * DT, DT, norm=1))
    phases.append(Phase("conv_out", DT, DT, feeds=2))
    ffn(1, 2)
    ffn(2, 3)
    phases.append(Phase("qkv", 3 * DT, DT, norm=4))
    phases.append(Phase("attn_out", DT, DT, feeds=5))
    ffn(3, 5)
    g = operands = pairs = hidden = made = 0
    rows = {8: 0, 6: 0}
    operands = DT
    x_first = 0
    for n, p in enumerate(phases):
        p.before = phases[n - 1] if n else None
        p.after = phases[n + 1] if n + 1 < len(phases) else None
        p.g = g
        g += p.tiles
        p.row = rows[p.k]
        rows[p.k] += p.tiles
        p.pairs = pairs
        p.hidden = hidden
        p.made = made
        if p.kind in ("up", "conv_in", "qkv"):
            p.needs = x_first
            p.makes = operands
            n_made = p.tiles // 2 if p.kind == "up" else DT
            if p.kind == "up":
                pairs += n_made
            hidden += n_made
            made += n_made if p.kind != "qkv" else 0
            operands += n_made
        else:
            p.needs = phases[n - 1].makes
            p.makes = operands
            if p.feeds is not None and p.feeds < N_NORM - 1:
                x_first = operands
                operands += DT
    return phases, g, rows


PHASES, N_TILES, ROWS = plan()


def user_before(p, tile):
    if p.rot == 3:
        return 3 if tile >= 3 else W_SLOTS
    return 3 if tile < 3 and p.before is not None and p.before.rot == 3 else W_SLOTS


def psum_user_before(p, tile):
    if p.kind == "qkv" or (tile < 2 and p.before is not None and p.before.kind == "qkv"):
        return 2
    return user_before(p, tile)


def streaming_conv_chunkattn_macaron(nc, x_t, w8, w6, gains, conv_taps, conv_state, cache_kt, cache_v,
                                     bias_ext, ident_in, y_t, conv_out_state, k_t, v_t):
    with ExitStack() as ctx:
        def sb(name, shape, dt=F32):
            return ctx.enter_context(nc.sbuf_tensor(name, shape, dt))

        def sem(name):
            return ctx.enter_context(nc.semaphore(name))

        x = sb("x", [P, DT, TOK])
        xg_hi = sb("xg_hi", [P, DT, TOK], F32R)
        xg_lo = sb("xg_lo", [P, DT, TOK], F32R)
        hid_hi = sb("hid_hi", [P, DT, TOK], F32R)
        hid_lo = sb("hid_lo", [P, DT, TOK], F32R)
        w_raw = sb("w_raw", [P, RAW_SLOTS, DT * P])
        w_hi = sb("w_hi", [P, W_SLOTS, DT * P], F32R)
        w_lo = sb("w_lo", [P, W_SLOTS, DT * P], F32R)
        rstd = sb("rstd", [P, TOK])
        sumsq = sb("sumsq", [P, TOK])
        sq = sb("sq", [P, 2, TOK])
        scaled = sb("scaled", [P, TOK])
        scaled2 = sb("scaled2", [P, TOK])
        silu = sb("silu", [P, TOK])
        hidden = sb("hidden", [P, TOK])
        gain = sb("gain", [P, N_NORM, DT])
        taps = sb("taps", [P, 3, DT])
        eps = sb("eps", [P, 1])
        ones = sb("ones", [P, P])
        ident = sb("ident", [P, P])
        state_in = sb("state_in", [P, DT, CONV_PAD])
        state_out = sb("state_out", [P, DT, 2 * CONV_PAD])
        ue = sb("ue", [P, 2, UE])
        conv_y = sb("conv_y", [P, UE - CONV_PAD])
        q_t = sb("q_t", [P, 2, TOK])
        k_sb = sb("k_sb", [P, 2, TOK])
        v_sb = sb("v_sb", [P, 2, TOK])
        v_tok = sb("v_tok", [P, QT + 1, P])
        kc = sb("kc", [P, 2, PAST])
        vc = sb("vc", [P, 2, P])
        bias = sb("bias", [P, 2, BIAS_W])
        scores = sb("scores", [P, 2, BIAS_W])
        probs = sb("probs", [P, PROB_SLOTS, BIAS_W])
        probs_t = sb("probs_t", [P, 2, BIAS_W])
        row_max = sb("row_max", [P, UNITS])
        neg_max = sb("neg_max", [P, UNITS])
        row_sum = sb("row_sum", [P, UNITS])
        inv_sum = sb("inv_sum", [P, UNITS])
        ps = ctx.enter_context(nc.psum_tensor("ps", [P, 8, 512], F32))

        x_loaded = [sem(f"x_loaded{m}") for m in range(DT)]
        gain_loaded = sem("gain_loaded")
        consts_loaded = sem("consts_loaded")
        raw_loaded = [sem(f"raw_loaded{s}") for s in range(RAW_SLOTS)]
        w_hi_done = sem("w_hi_done")
        w_split = sem("w_split")
        tile_done = sem("tile_done")
        tile_read = sem("tile_read")
        setup_done = sem("setup_done")
        operand_ready = sem("operand_ready")
        xg_hi_done = sem("xg_hi_done")
        sq_done = sem("sq_done")
        sq_added = sem("sq_added")
        sumsq_done = sem("sumsq_done")
        rms_done = sem("rms_done")
        rstd_done = sem("rstd_done")
        silu_done = sem("silu_done")
        hidden_made = sem("hidden_made")
        hidden_hi_done = sem("hidden_hi_done")
        u_made = sem("u_made")
        state_set = sem("state_set")
        tap0_done = sem("tap0_done")
        taps_done = sem("taps_done")
        state_kept = sem("state_kept")
        kv_stored = [sem(f"kv_stored{s}") for s in range(2)]
        bias_loaded = [sem(f"bias_loaded{s}") for s in range(2)]
        cache_loaded = [sem(f"cache_loaded{s}") for s in range(2)]
        scores_done = sem("scores_done")
        scores_read = sem("scores_read")
        neg_max_done = sem("neg_max_done")
        exp_done = sem("exp_done")
        inv_sum_done = sem("inv_sum_done")
        probs_ready = sem("probs_ready")
        turned = sem("turned")
        turned_read = sem("turned_read")
        pv_done = sem("pv_done")
        y_made = sem("y_made")
        out_scaled = sem("out_scaled")
        pool_y_made = sem("pool_y_made")
        stored = sem("stored")
        state_stored = sem("state_stored")

        def banks(slot):
            return ps[:, 2 * slot:2 * slot + 2, 0:HALF]

        def halves(ap):
            return ap.rearrange("p (b c) -> p b c", b=2)

        def sum_slot(n):
            return 0 if n == N_NORM - 1 else W_SLOTS - 1

        S_BANK, T_BANK, O_BANK, OS_BANK = 4, 5, 6, 7

        def ahead(p, at, tile):
            t = tile + AHEAD
            if t < p.tiles:
                return p, at.plus(AHEAD), t % p.rot, user_before(p, t)
            n = p.after
            if n is None:
                return None
            t -= p.tiles
            return n, At(n.g + t), t % n.rot, user_before(n, t)

        def unit_of(u):
            e, i = divmod(u, QT + 1)
            return e, i, PAST + DEC_SEQ if i == QT else P * (i + 1)

        def parity(t):
            return (t.of() if isinstance(t.i, int) else t.first) % 2

        def prob_slot(u, t):
            return (UNITS * parity(t) + u) % PROB_SLOTS

        TURN_LAG, PV_LAG = 3, 4
        LAST_SLOT = UNITS + PV_LAG
        SPLIT_AT = 3
        SLOT_AT = {(n * (3 * DT - 2)) // (LAST_SLOT - 1): n for n in range(LAST_SLOT)}
        assert len(SLOT_AT) == LAST_SLOT and LAST_SLOT <= 2 * (DT - 1)
        out_tiles = (scaled, scaled2)

        block = ctx.enter_context(nc.Block())

        @block.sync
        def _(sp):
            sp.sem_inc(w_split, RAW_SLOTS)
            sp.sem_inc(tile_done, W_SLOTS)
            sp.sem_inc(tile_read, W_SLOTS)
            sp.sem_inc(sq_added, 2)
            sp.sem_inc(scores_read, 1)
            sp.sem_inc(turned_read, 1)
            sp.sem_inc(pv_done, 2)
            for s in range(2):
                sp.sem_inc(kv_stored[s], 32)
            for p in PHASES:
                stream = w8 if p.k == 8 else w6
                with sp.Fori(0, p.tiles // RAW_SLOTS) as i:
                    for s in range(RAW_SLOTS):
                        at = At(p.g + s, RAW_SLOTS, i)
                        sp.wait_ge(w_split, at.of(1, 1))
                        row = At(p.row + s, RAW_SLOTS, i).of()
                        sp.dma_start(w_raw[:, s, 0:p.k * P], stream[bass.ds(row, 1)].rearrange("a p n -> p (a n)")
                                     ).then_inc(raw_loaded[s], 16)
            for n, m in enumerate(range(len(out_tiles), DT)):
                sp.wait_ge(y_made, n + 1)
                sp.dma_start(y_t[m], x[:, m, :]).then_inc(stored, 16)
            sp.wait_ge(stored, 16 * DT)
            sp.wait_ge(state_stored, 16)
            for s in range(2):
                sp.wait_ge(kv_stored[s], 32 + 32 * (DT // 2))

        @block.gpsimd
        def _(pool):
            pool.memset(ones[:, :], 1.0)
            pool.memset(eps[:, :], EPS)
            pool.memset(ue[:, :, 0:CONV_PAD], 0.0)
            pool.memset(bias[0:CHUNK, :, 0:CHUNK], MASKED).then_inc(setup_done, 1)
            pool.dma_start(taps[:, :, :], conv_taps).then_inc(consts_loaded, 16)
            pool.dma_start(state_in[:, :, :], conv_state).then_inc(consts_loaded, 16)
            pool.dma_start(ident[:, :], ident_in).then_inc(consts_loaded, 16)

            def sum_squares(n):
                for m in range(DT - 1 if n == N_NORM - 1 else DT):
                    pool.wait_ge(sq_done, DT * n + m + 1)
                    if m == 0:
                        if n:
                            pool.wait_ge(sumsq_done, n)
                        ins = pool.tensor_copy(sumsq[:, :], sq[:, 0, :])
                    else:
                        pool.wait_ge(sq_added, 2 + DT * n + m)
                        ins = pool.tensor_tensor(sumsq[:, :], sumsq[:, :], sq[:, m % 2, :], ALU.add)
                    ins.then_inc(sq_added, 1)

            def load_bias(t, e):
                h = 2 * t + e
                row = bias_ext[h]
                for first, end, left in ((0, CHUNK, CHUNK), (CHUNK, P, 0)):
                    src = bass.AP(tensor=row.tensor, offset=row.offset + first + left,
                                  ap=[[1, end - first], [1, BIAS_W - left]])
                    pool.dma_start(bias[first:end, e, left:BIAS_W], src).then_inc(bias_loaded[e], 16)

            def load_cache(t):
                pool.dma_start(kc[:, t % 2, :], cache_kt[t]).then_inc(cache_loaded[t % 2], 16)
                pool.dma_start(vc[:, t % 2, :], cache_v[t]).then_inc(cache_loaded[t % 2], 16)

            pool.wait_ge(setup_done, 1)
            for e in range(2):
                load_bias(0, e)
            for t in range(2):
                load_cache(t)
            for p in PHASES:
                if p.norm:
                    sum_squares(p.norm)
                if p.kind == "conv_out":
                    pool.wait_ge(state_kept, DT)
                    pool.dma_start(conv_out_state, state_out[:, :, :]).then_inc(state_stored, 16)
                if p.kind == "qkv":
                    for t in range(DT):
                        if t >= 1:
                            for e in range(2):
                                pool.wait_ge(scores_read, 1 + UNITS * (t - 1) + (QT + 1) * (e + 1))
                                load_bias(t, e)
                            if t >= 2:
                                pool.wait_ge(pv_done, 2 + UNITS * (t - 1))
                                load_cache(t)
            sum_squares(N_NORM - 1)
            pool.wait_ge(rstd_done, N_NORM)
            for m, tile in enumerate(out_tiles):
                pool.wait_ge(out_scaled, m + 1)
                pool.tensor_tensor(tile[:, :], tile[:, :], rstd[:, :], ALU.mult).then_inc(pool_y_made, 1)

        @block.scalar
        def _(act):
            def split_hi(nxt):
                if nxt is None:
                    return
                p, at, slot, back = nxt
                raw = at.first % RAW_SLOTS
                act.wait_ge(raw_loaded[raw], at.half().of(16, 16))
                act.wait_ge(tile_done, at.of(1, W_SLOTS - back + 1))
                act.activation(w_hi[:, slot, 0:p.k * P], w_raw[:, raw, 0:p.k * P], ACT.Copy).then_inc(w_hi_done, 1)

            def xg_upper(n, m):
                act.activation(xg_hi[:, m, :], x[:, m, :], ACT.Copy, scale=gain[:, n, m:m + 1]).then_inc(xg_hi_done, 1)

            def squares(n, m):
                act.wait_ge(sq_added, DT * n + m + 1)
                act.activation(sq[:, m % 2, :], x[:, m, :], ACT.Square).then_inc(sq_done, 1)

            def root(n):
                act.wait_ge(sumsq_done, n + 1)
                if n == 0:
                    act.wait_ge(setup_done, 1)
                act.activation(halves(rstd[:, :]), banks(sum_slot(n)), ACT.Sqrt,
                               bias=eps[:, :], scale=1.0 / D_MODEL).then_inc(rms_done, 1)

            def split_hidden(tile, made):
                act.wait_ge(hidden_made, made.of(1, 1))
                act.activation(hid_hi[:, bass.ds(tile, 1), :].rearrange("p a n -> p (a n)"), hidden[:, :],
                               ACT.Copy).then_inc(hidden_hi_done, 1)

            def attend(slot, t):
                if slot == 1:
                    for n, (bank, out) in enumerate(((T_BANK, v_tok[:, 0:QT, :].rearrange("p a n -> p (a n)")),
                                                     (OS_BANK, v_tok[0:DEC_SEQ, QT, :]))):
                        act.wait_ge(turned, t.of(UNITS + 2, n + 1))
                        rows = P if n == 0 else DEC_SEQ
                        act.activation(out, ps[0:rows, bank, 0:out.shape[1]], ACT.Copy).then_inc(turned_read, 1)
                u = slot - TURN_LAG
                if 0 <= u < UNITS:
                    e, i, width = unit_of(u)
                    act.wait_ge(turned, t.of(UNITS + 2, u + 3))
                    act.wait_ge(pv_done, t.of(UNITS, u + 1))
                    if i < QT:
                        act.activation(probs_t[:, u % 2, 0:width], ps[:, T_BANK, 0:width],
                                       ACT.Copy).then_inc(turned_read, 1)
                    else:
                        act.activation(probs_t[:, u % 2, 0:P], ps[:, T_BANK, 0:P], ACT.Copy)
                        act.activation(probs_t[0:DEC_SEQ, u % 2, P:2 * P], ps[0:DEC_SEQ, T_BANK, P:2 * P],
                                       ACT.Copy).then_inc(turned_read, 1)
                u = slot
                if u < UNITS:
                    e, i, width = unit_of(u)
                    act.wait_ge(neg_max_done, t.of(UNITS, u + 1))
                    act.activation(probs[:, prob_slot(u, t), 0:width], scores[:, u % 2, 0:width], ACT.Exp,
                                   bias=neg_max[:, u:u + 1], scale=1.0,
                                   accum_out=row_sum[:, u:u + 1]).then_inc(exp_done, 1)

            def attended(t):
                act.wait_ge(pv_done, t.of(UNITS, 2 + UNITS))
                tile = bass.ds(t.of(), 1)
                act.activation(hid_hi[:, tile, 0:SEQ].rearrange("p a n -> p (a n)"), ps[:, O_BANK, :], ACT.Copy)
                act.activation(hid_hi[:, tile, SEQ:TOK].rearrange("p a n -> p (a n)"), ps[:, OS_BANK, 0:DEC_SEQ],
                               ACT.Copy).then_inc(hidden_hi_done, 1)

            act.preload_act_table(ACT.Silu)
            act.dma_start(gain[:, :, :], gains).then_inc(gain_loaded, 16)
            for m in range(DT):
                act.dma_start(x[:, m, :], x_t[m]).then_inc(x_loaded[m], 16)
            act.wait_ge(gain_loaded, 16)
            for m in range(DT):
                act.wait_ge(x_loaded[m], 16)
                xg_upper(0, m)
                if m == 0:
                    split_hi((PHASES[0], At(0), 0, W_SLOTS))
            for t in range(1, AHEAD):
                split_hi((PHASES[0], At(t), t, W_SLOTS))
            for m in range(DT):
                squares(0, m)

            def up(p, i, tiles):
                for u in tiles:
                    at = At(p.g + u, 4, i)
                    split_hi(ahead(p, at, u + 4 * i if isinstance(i, int) else u))
                    if p.norm is not None and isinstance(i, int) and i == 0 and u == 0:
                        root(p.norm)
                    if u % 2 == 0:
                        act.wait_ge(tile_read, at.of(1, W_SLOTS + 1))
                        act.activation(silu[:, :], scaled[:, :], ACT.Silu).then_inc(silu_done, 1)
                    else:
                        split_hidden(At(u // 2, 2, i).of(), At(p.made + u // 2, 2, i))

            def down(p):
                for m in range(DT):
                    at = At(p.g + m)
                    split_hi(ahead(p, at, m))
                    if p.feeds == N_NORM - 1 and m == 0:
                        act.preload_act_table(ACT.Sqrt)
                    if p.feeds is not None:
                        act.wait_ge(tile_read, at.of(1, W_SLOTS + 1))
                        if p.feeds < N_NORM - 1:
                            xg_upper(p.feeds, m)
                        squares(p.feeds, m)

            def conv(p, i, js):
                if isinstance(i, int) and i == 0:
                    act.wait_ge(consts_loaded, 48)
                for jj in js:
                    j = At(jj, 2, i)
                    slot = jj % 2
                    for r in range(3):
                        at = At(p.g + 3 * jj + r, 6, i)
                        split_hi(ahead(p, at, 3 * jj + r + (6 * i if isinstance(i, int) else 0)))
                        if r == 0:
                            if p.norm is not None and isinstance(i, int) and i == 0 and jj == 0:
                                root(p.norm)
                            act.activation(ue[:, slot, CONV_PAD + SEQ:2 * CONV_PAD + SEQ],
                                           state_in[:, bass.ds(j.of(), 1), :].rearrange("p a n -> p (a n)"),
                                           ACT.Copy).then_inc(state_set, 1)
                        if r == 1:
                            act.wait_ge(u_made, j.of(1, 1))
                            act.wait_ge(state_set, j.of(1, 1))
                            act.activation(conv_y[:, :], ue[:, slot, 0:UE - CONV_PAD], ACT.Copy,
                                           scale=taps[:, 0, bass.ds(j.of(), 1)]).then_inc(tap0_done, 1)
                            so = state_out[:, bass.ds(j.of(), 1), :].rearrange("p a n -> p (a n)")
                            act.activation(so[:, 0:CONV_PAD], ue[:, slot, SEQ:SEQ + CONV_PAD], ACT.Copy)
                            act.activation(so[:, CONV_PAD:2 * CONV_PAD], ue[:, slot, UE - CONV_PAD:UE],
                                           ACT.Copy).then_inc(state_kept, 1)
                        if r == 2:
                            split_hidden(j.of(), At(p.made + jj, 2, i))

            def qkv(p, t, with_attention):
                before = t.plus(-1)
                for r in range(3):
                    for k in range(DT):
                        slot = SLOT_AT.get(DT * r + k - 1) if with_attention else None
                        if k == 0 and r > 0:
                            first_root(p, t, r - 1)
                        if slot is not None:
                            attend(slot, before)
                        if k == (1 if r else SPLIT_AT) and (r > 0 or with_attention):
                            finish_tile(p, t if r else before, (r - 1) % 3)
                if with_attention:
                    attended(before)

            def first_root(p, t, r):
                if isinstance(t.i, int) and t.of() == 0 and r == 0:
                    root(p.norm)

            def finish_tile(p, t, r):
                local = 3 * t.first + r
                at = At(p.g + local, 3 * t.step, t.i)
                if not isinstance(t.i, int):
                    split_hi(ahead(p, at, local))
                else:
                    split_hi(ahead(p, At(p.g + 3 * t.of() + r), 3 * t.of() + r))
                if r == 2:
                    act.wait_ge(tile_read, at.of(1, W_SLOTS + 1))
                    odd = t.first % 2 if not isinstance(t.i, int) else t.of() % 2
                    for src, dst in ((k_sb, k_t), (v_sb, v_t)):
                        act.dma_start(dst[bass.ds(t.of(), 1)].rearrange("a p n -> p (a n)"), src[:, odd, :]
                                      ).then_inc(kv_stored[odd], 16)

            for p in PHASES:
                if p.kind == "up":
                    n = p.tiles // 4
                    up(p, 0, range(4))
                    if n > 2:
                        with act.Fori(1, n - 1) as i:
                            up(p, i, range(4))
                    up(p, n - 1, range(4))
                elif p.kind == "conv_in":
                    n = p.tiles // 6
                    conv(p, 0, range(2))
                    with act.Fori(1, n - 1) as i:
                        conv(p, i, range(2))
                    conv(p, n - 1, range(2))
                elif p.kind == "qkv":
                    qkv(p, At(0), False)
                    with act.Fori(0, (DT - 2) // 2) as i:
                        qkv(p, At(1, 2, i), True)
                        qkv(p, At(2, 2, i), True)
                    qkv(p, At(DT - 1), True)
                    finish_tile(p, At(DT - 1), 2)
                    for slot in range(LAST_SLOT):
                        attend(slot, At(DT - 1))
                    attended(At(DT - 1))
                else:
                    down(p)
            for m, tile in enumerate(out_tiles):
                act.activation(tile[:, :], x[:, m, :], ACT.Copy, scale=gain[:, N_NORM - 1, m:m + 1]).then_inc(out_scaled, 1)
            root(N_NORM - 1)
            for m, tile in enumerate(out_tiles):
                act.wait_ge(pool_y_made, m + 1)
                act.dma_start(y_t[m], tile[:, :]).then_inc(stored, 16)

        @block.vector
        def _(dve):
            def split_lo(nxt):
                if nxt is None:
                    return
                p, at, slot, back = nxt
                raw = at.first % RAW_SLOTS
                dve.wait_ge(w_hi_done, at.of(1, 1))
                dve.tensor_tensor(w_lo[:, slot, 0:p.k * P], w_raw[:, raw, 0:p.k * P],
                                  w_hi[:, slot, 0:p.k * P].bitcast(F32), ALU.subtract).then_inc(w_split, 1)

            def norm_lo(n, m):
                dve.wait_ge(xg_hi_done, DT * n + m + 1)
                dve.scalar_tensor_tensor(xg_lo[:, m, :], x[:, m, :], gain[:, n, m:m + 1], xg_hi[:, m, :].bitcast(F32),
                                         ALU.mult, ALU.subtract).then_inc(operand_ready, 1)

            def invert(n):
                dve.wait_ge(rms_done, n + 1)
                dve.reciprocal(rstd[:, :], rstd[:, :]).then_inc(rstd_done, 1)
                dve.wait_ge(rstd_done, n + 1)

            def split_hidden(tile, made):
                dve.wait_ge(hidden_hi_done, made.of(1, 1))
                dve.tensor_tensor(hid_lo[:, bass.ds(tile, 1), :].rearrange("p a n -> p (a n)"), hidden[:, :],
                                  hid_hi[:, bass.ds(tile, 1), :].rearrange("p a n -> p (a n)").bitcast(F32),
                                  ALU.subtract).then_inc(operand_ready, 1)

            def attend(slot, t):
                u = slot
                if u < UNITS:
                    e, i, width = unit_of(u)
                    if u % (QT + 1) == 0:
                        dve.wait_ge(bias_loaded[e], t.of(32, 32))
                    dve.wait_ge(scores_done, t.of(UNITS, u + 1))
                    dve.tensor_tensor(scores[:, u % 2, 0:width], ps[:, S_BANK, 0:width],
                                      bias[:, e, 0:width][:, ::-1], ALU.add).then_inc(scores_read, 1)
                    dve.wait_ge(scores_read, t.of(UNITS, 1 + u + 1))
                    dve.tensor_reduce(neg_max[:, u:u + 1], scores[:, u % 2, 0:width],
                                      mybir.AxisListType.X, ALU.max, negate=True).then_inc(neg_max_done, 1)
                u = slot - 1
                if 0 <= u < UNITS:
                    e, i, width = unit_of(u)
                    dve.wait_ge(exp_done, t.of(UNITS, u + 1))
                    dve.reciprocal(inv_sum[:, u:u + 1], row_sum[:, u:u + 1]).then_inc(inv_sum_done, 1)
                    dve.wait_ge(inv_sum_done, t.of(UNITS, u + 1))
                    dve.tensor_scalar(probs[:, prob_slot(u, t), 0:width], probs[:, prob_slot(u, t), 0:width],
                                      inv_sum[:, u:u + 1], None, ALU.mult).then_inc(probs_ready, 1)

            def attended(p, t):
                tile = bass.ds(t.of(), 1)
                dve.wait_ge(hidden_hi_done, t.of(1, p.hidden + 1))
                dve.tensor_tensor(hid_lo[:, tile, 0:SEQ].rearrange("p a n -> p (a n)"), ps[:, O_BANK, :],
                                  hid_hi[:, tile, 0:SEQ].rearrange("p a n -> p (a n)").bitcast(F32), ALU.subtract)
                dve.tensor_tensor(hid_lo[:, tile, SEQ:TOK].rearrange("p a n -> p (a n)"), ps[:, OS_BANK, 0:DEC_SEQ],
                                  hid_hi[:, tile, SEQ:TOK].rearrange("p a n -> p (a n)").bitcast(F32),
                                  ALU.subtract).then_inc(operand_ready, 1)

            dve.wait_ge(gain_loaded, 16)
            for m in range(DT):
                norm_lo(0, m)
                if m == 0:
                    split_lo((PHASES[0], At(0), 0, W_SLOTS))
            for t in range(1, AHEAD):
                split_lo((PHASES[0], At(t), t, W_SLOTS))
            for m in range(DT):
                dve.wait_ge(sq_done, m + 1)
                if m == 0:
                    ins = dve.tensor_copy(sumsq[:, :], sq[:, 0, :])
                else:
                    dve.wait_ge(sq_added, 2 + m)
                    ins = dve.tensor_tensor(sumsq[:, :], sumsq[:, :], sq[:, m % 2, :], ALU.add)
                ins.then_inc(sq_added, 1)

            def up(p, i, tiles):
                for u in tiles:
                    at = At(p.g + u, 4, i)
                    if p.norm is not None and isinstance(i, int) and i == 0 and u == 0:
                        split_lo(ahead(p, at, 0))
                        invert(p.norm)
                    dve.wait_ge(tile_done, at.of(1, W_SLOTS + 1))
                    out = scaled if u % 2 == 0 else scaled2
                    dve.tensor_tensor(halves(out[:, :]), banks(u), halves(rstd[:, :]), ALU.mult).then_inc(tile_read, 1)
                    if u % 2:
                        dve.wait_ge(silu_done, At(p.pairs + u // 2, 2, i).of(1, 1))
                        dve.wait_ge(tile_read, at.of(1, W_SLOTS + 1))
                        dve.tensor_tensor(hidden[:, :], silu[:, :], scaled2[:, :], ALU.mult).then_inc(hidden_made, 1)
                    if not (p.norm is not None and isinstance(i, int) and i == 0 and u == 0):
                        split_lo(ahead(p, at, u + 4 * i if isinstance(i, int) else u))
                    if u % 2:
                        split_hidden(At(u // 2, 2, i).of(), At(p.hidden + u // 2, 2, i))

            def down(p):
                share = 0.5 if p.kind == "down" else 1.0
                for m in range(DT):
                    at = At(p.g + m)
                    dve.wait_ge(tile_done, at.of(1, W_SLOTS + 1))
                    dve.scalar_tensor_tensor(halves(x[:, m, :]), banks(m % W_SLOTS), share, halves(x[:, m, :]),
                                             ALU.mult, ALU.add).then_inc(tile_read, 1)
                    split_lo(ahead(p, at, m))
                    if p.feeds is not None and p.feeds < N_NORM - 1:
                        norm_lo(p.feeds, m)

            def conv(p, i, js):
                for jj in js:
                    j = At(jj, 2, i)
                    slot = jj % 2
                    for r in range(3):
                        at = At(p.g + 3 * jj + r, 6, i)
                        first = isinstance(i, int) and i == 0 and jj == 0 and r == 0
                        if first:
                            dve.wait_ge(consts_loaded, 48)
                            dve.wait_ge(setup_done, 1)
                        nxt = ahead(p, at, 3 * jj + r + (6 * i if isinstance(i, int) else 0))
                        if first:
                            invert(p.norm)
                        dve.wait_ge(tile_done, at.of(1, W_SLOTS + 1))
                        if r == 0:
                            dve.tensor_tensor(halves(scaled[:, :]), banks(r), halves(rstd[:, :]),
                                              ALU.mult).then_inc(tile_read, 1)
                            split_lo(nxt)
                        if r == 1:
                            dve.wait_ge(tile_read, at.of(1, W_SLOTS))
                            dve.tensor_tensor(halves(scaled2[:, :]), banks(r), halves(scaled[:, :]),
                                              ALU.mult).then_inc(tile_read, 1)
                            dve.wait_ge(tile_read, at.of(1, W_SLOTS + 1))
                            dve.tensor_tensor(ue[:, slot, CONV_PAD:CONV_PAD + SEQ], scaled2[:, 0:SEQ],
                                              rstd[:, 0:SEQ], ALU.mult)
                            dve.tensor_tensor(ue[:, slot, 2 * CONV_PAD + SEQ:UE], scaled2[:, SEQ:TOK],
                                              rstd[:, SEQ:TOK], ALU.mult).then_inc(u_made, 1)
                            split_lo(nxt)
                            dve.wait_ge(tap0_done, j.of(1, 1))
                            for k in range(1, 3):
                                if k == 2:
                                    dve.wait_ge(taps_done, j.of(2, 1))
                                dve.scalar_tensor_tensor(conv_y[:, :], ue[:, slot, k:k + UE - CONV_PAD],
                                                         taps[:, k, bass.ds(j.of(), 1)], conv_y[:, :],
                                                         ALU.mult, ALU.add).then_inc(taps_done, 1)
                        if r == 2:
                            dve.tensor_tensor(halves(silu[:, :]), banks(r), halves(rstd[:, :]),
                                              ALU.mult).then_inc(tile_read, 1)
                            dve.wait_ge(tile_read, at.of(1, W_SLOTS + 1))
                            dve.wait_ge(taps_done, j.of(2, 2))
                            dve.tensor_tensor(hidden[:, 0:SEQ], silu[:, 0:SEQ], conv_y[:, 0:SEQ], ALU.mult)
                            dve.tensor_tensor(hidden[:, SEQ:TOK], silu[:, SEQ:TOK],
                                              conv_y[:, SEQ + CONV_PAD:UE - CONV_PAD], ALU.mult
                                              ).then_inc(hidden_made, 1)
                            split_lo(nxt)
                            split_hidden(j.of(), At(p.hidden + jj, 2, i))

            def qkv(p, t, with_attention):
                before = t.plus(-1)
                for r in range(3):
                    for k in range(DT):
                        slot = SLOT_AT.get(DT * r + k - 1) if with_attention else None
                        if k == 0 and r > 0:
                            read_tile(p, t, r - 1)
                        if slot is not None:
                            attend(slot, before)
                        if k == (1 if r else SPLIT_AT) and (r > 0 or with_attention):
                            split_ahead(p, t if r else before, (r - 1) % 3)
                if with_attention:
                    attended(p, before)
                read_tile(p, t, 2)

            def place(p, t, r):
                if isinstance(t.i, int):
                    return 3 * t.of() + r, At(p.g + 3 * t.of() + r), t.of() % 2
                return 3 * t.first + r, At(p.g + 3 * t.first + r, 3 * t.step, t.i), t.first % 2

            def split_ahead(p, t, r):
                local, at, odd = place(p, t, r)
                split_lo(ahead(p, at, local))

            def read_tile(p, t, r):
                local, at, odd = place(p, t, r)
                if isinstance(t.i, int) and t.of() == 0 and r == 0:
                    invert(p.norm)
                dve.wait_ge(tile_done, at.of(1, W_SLOTS + 1))
                if r == 1:
                    dve.wait_ge(kv_stored[odd], t.half().of(32, 32))
                out = (q_t, k_sb, v_sb)[r]
                dve.scalar_tensor_tensor(halves(out[:, odd, :]), banks(local % 2), HEAD_DIM ** -0.5 if r == 0 else 1.0,
                                         halves(rstd[:, :]), ALU.mult, ALU.mult).then_inc(tile_read, 1)

            for p in PHASES:
                if p.kind == "up":
                    n = p.tiles // 4
                    up(p, 0, range(4))
                    if n > 2:
                        with dve.Fori(1, n - 1) as i:
                            up(p, i, range(4))
                    up(p, n - 1, range(4))
                elif p.kind == "conv_in":
                    n = p.tiles // 6
                    conv(p, 0, range(2))
                    with dve.Fori(1, n - 1) as i:
                        conv(p, i, range(2))
                    conv(p, n - 1, range(2))
                elif p.kind == "qkv":
                    qkv(p, At(0), False)
                    with dve.Fori(0, (DT - 2) // 2) as i:
                        qkv(p, At(1, 2, i), True)
                        qkv(p, At(2, 2, i), True)
                    qkv(p, At(DT - 1), True)
                    split_ahead(p, At(DT - 1), 2)
                    for slot in range(LAST_SLOT):
                        attend(slot, At(DT - 1))
                    attended(p, At(DT - 1))
                else:
                    down(p)
            invert(N_NORM - 1)
            for m in range(len(out_tiles), DT):
                dve.scalar_tensor_tensor(x[:, m, :], x[:, m, :], gain[:, N_NORM - 1, m:m + 1], rstd[:, :],
                                         ALU.mult, ALU.mult).then_inc(y_made, 1)

        @block.tensor
        def _(pe):
            def product(p, at, w_slot, out_slot, back, operand, wait_operand, between=None, ks=None):
                hi, lo = operand
                pe.wait_ge(w_split, at.of(1, RAW_SLOTS + 1))
                pe.wait_ge(tile_read, at.of(1, W_SLOTS - back + 1))
                for k in ks or range(p.k):
                    if wait_operand:
                        pe.wait_ge(operand_ready, p.needs + k + 1)
                    w = slice(k * P, (k + 1) * P)
                    for n, (wt, xt) in enumerate(((w_hi, hi), (w_hi, lo), (w_lo, hi))):
                        for b in range(2):
                            mm = pe.matmul(ps[:, 2 * out_slot + b, 0:HALF], wt[:, w_slot, w],
                                           xt[:, k, b * HALF:(b + 1) * HALF],
                                           start=(k == 0 and n == 0), stop=(k == p.k - 1 and n == 2))
                    if k == p.k - 1:
                        mm.then_inc(tile_done, 1)
                    elif between is not None:
                        between(k)

            def sum_over_partitions(n):
                if n == 0:
                    pe.wait_ge(setup_done, 1)
                final = n == N_NORM - 1
                pe.wait_ge(sq_added, 2 + DT * (n + 1) - final)
                for b in range(2):
                    mm = pe.matmul(ps[:, 2 * sum_slot(n) + b, 0:HALF], ones[:, :],
                                   sumsq[:, b * HALF:(b + 1) * HALF], start=True, stop=not final)
                if final:
                    pe.wait_ge(sq_done, DT * (n + 1))
                    for b in range(2):
                        mm = pe.matmul(ps[:, 2 * sum_slot(n) + b, 0:HALF], ones[:, :],
                                       sq[:, (DT - 1) % 2, b * HALF:(b + 1) * HALF], start=False, stop=True)
                mm.then_inc(sumsq_done, 1)

            mixer = next(p for p in PHASES if p.kind == "qkv")

            def attend(slot, t, odd):
                if slot == 1:
                    if not (isinstance(t.i, int) and t.of() == 0):
                        pe.wait_ge(operand_ready, t.of(1, mixer.makes))
                    pe.wait_ge(tile_read, t.of(3, W_SLOTS + mixer.g + 3))
                    pe.wait_ge(turned_read, t.of(UNITS + 2, 1))
                    for c in range(QT):
                        mm = pe.transpose(ps[:, T_BANK, c * P:(c + 1) * P], v_sb[:, odd, c * P:(c + 1) * P],
                                          ident[:, :])
                    mm.then_inc(turned, 1)
                    pe.transpose(ps[0:DEC_SEQ, OS_BANK, 0:P], v_sb[:, odd, SEQ:TOK], ident[:, :]).then_inc(turned, 1)
                u = slot - TURN_LAG
                if 0 <= u < UNITS:
                    e, i, width = unit_of(u)
                    pe.wait_ge(probs_ready, t.of(UNITS, u + 1))
                    pe.wait_ge(turned_read, t.of(UNITS + 2, u + 3))
                    if i < QT:
                        for c in range(i + 1):
                            mm = pe.transpose(ps[:, T_BANK, c * P:(c + 1) * P],
                                              probs[:, prob_slot(u, t), c * P:(c + 1) * P], ident[:, :])
                    else:
                        pe.transpose(ps[:, T_BANK, 0:P], probs[:, prob_slot(u, t), 0:PAST], ident[:, :])
                        mm = pe.transpose(ps[0:DEC_SEQ, T_BANK, P:2 * P],
                                          probs[:, prob_slot(u, t), PAST:width], ident[:, :])
                    mm.then_inc(turned, 1)
                u = slot - PV_LAG
                if 0 <= u < UNITS:
                    e, i, width = unit_of(u)
                    hd = slice(HEAD_DIM * e, HEAD_DIM * (e + 1))
                    pe.wait_ge(turned_read, t.of(UNITS + 2, 1 + u + 3))
                    if i < QT:
                        for c in range(i + 1):
                            mm = pe.matmul(ps[hd, O_BANK, i * P:(i + 1) * P], v_tok[:, c, hd],
                                           probs_t[:, u % 2, c * P:(c + 1) * P], start=(c == 0), stop=(c == i))
                    else:
                        pe.matmul(ps[hd, OS_BANK, 0:DEC_SEQ], vc[:, odd, hd], probs_t[:, u % 2, P - DEC_SEQ:P],
                                  start=True, stop=False)
                        mm = pe.matmul(ps[hd, OS_BANK, 0:DEC_SEQ], v_tok[0:DEC_SEQ, QT, hd],
                                       probs_t[0:DEC_SEQ, u % 2, 2 * P - DEC_SEQ:2 * P], start=False, stop=True)
                    mm.then_inc(pv_done, 1)
                u = slot
                if u < UNITS:
                    e, i, width = unit_of(u)
                    hd = slice(HEAD_DIM * e, HEAD_DIM * (e + 1))
                    pe.wait_ge(scores_read, t.of(UNITS, u + 1))
                    if u == 0:
                        pe.wait_ge(tile_read, t.of(3, W_SLOTS + mixer.g + 2))
                        pe.wait_ge(cache_loaded[odd], t.half().of(32, 32))
                    if i < QT:
                        mm = pe.matmul(ps[:, S_BANK, 0:width], q_t[hd, odd, i * P:(i + 1) * P],
                                       k_sb[hd, odd, 0:width], start=True, stop=True)
                    else:
                        pe.matmul(ps[:, S_BANK, 0:PAST], q_t[hd, odd, TOK - P:TOK], kc[hd, odd, :],
                                  start=True, stop=True)
                        mm = pe.matmul(ps[:, S_BANK, PAST:width], q_t[hd, odd, TOK - P:TOK],
                                       k_sb[hd, odd, SEQ:TOK], start=True, stop=True)
                    mm.then_inc(scores_done, 1)

            def qkv(p, t, with_attention):
                odd = (t.of() if isinstance(t.i, int) else t.first) % 2
                before = t.plus(-1)
                first = isinstance(t.i, int) and t.of() == 0
                for r in range(3):
                    at = At(p.g + 3 * t.first + r, 3 * t.step, t.i)

                    def between(k):
                        slot = SLOT_AT.get(DT * r + k)
                        if slot is not None:
                            attend(slot, before, 1 - odd)

                    w_slot = (3 * t.first + r) % 3
                    product(p, at, w_slot, (3 * t.first + r) % 2, 2, (xg_hi, xg_lo), first and r == 0,
                            between if with_attention else None)
                    if first and r == 0:
                        sum_over_partitions(p.norm)
                    if with_attention:
                        between(DT - 1)

            def tiles(p, operand, i, n, wait_operand):
                for u in range(n):
                    peeled = isinstance(i, int)
                    local = u + n * i if peeled else u
                    psum_back = user_before(p, local) if peeled else p.rot
                    if peeled and p.norm is not None and local == sum_slot(p.norm):
                        pe.wait_ge(rms_done, p.norm + 1)
                    product(p, At(p.g + u, n, i), u % p.rot, u % p.rot, psum_back, operand, wait_operand and u == 0)
                    if peeled and p.norm is not None and local == (1 if p.norm == 0 else 0):
                        sum_over_partitions(p.norm)

            for p in PHASES:
                if p.kind == "up":
                    tiles(p, (xg_hi, xg_lo), 0, 4, p.norm is not None)
                    with pe.Fori(1, p.tiles // 4) as i:
                        tiles(p, (xg_hi, xg_lo), i, 4, False)
                elif p.kind == "conv_in":
                    tiles(p, (xg_hi, xg_lo), 0, 6, True)
                    with pe.Fori(1, p.tiles // 6) as i:
                        tiles(p, (xg_hi, xg_lo), i, 6, False)
                elif p.kind == "qkv":
                    qkv(p, At(0), False)
                    pe.wait_ge(consts_loaded, 48)
                    with pe.Fori(0, (DT - 2) // 2) as i:
                        qkv(p, At(1, 2, i), True)
                        qkv(p, At(2, 2, i), True)
                    qkv(p, At(DT - 1), True)
                    n, hid = p.after, (hid_hi, hid_lo)
                    for tile in range(2):
                        product(n, At(n.g + tile), tile, tile, 2, hid, tile == 0,
                                lambda k: attend((DT - 1) * tile + k, At(DT - 1), (DT - 1) % 2), range(DT - 1))
                    for tile in range(2):
                        product(n, At(n.g + tile), tile, tile, 2, hid, True, None, (DT - 1,))
                elif p.kind == "down":
                    with pe.Fori(0, p.tiles // 4) as i:
                        tiles(p, (hid_hi, hid_lo), i, 4, True)
                else:
                    for tile in range(2 if p.kind == "attn_out" else 0, p.tiles):
                        product(p, At(p.g + tile), tile % W_SLOTS, tile % W_SLOTS, psum_user_before(p, tile),
                                (hid_hi, hid_lo), tile == 0)
            sum_over_partitions(N_NORM - 1)


def weight_tiles(w):
    k, m = w.shape[0] // P, w.shape[1] // P
    return w.reshape(k, P, m, P).transpose(2, 1, 0, 3).reshape(m, P, k * P)


def interleaved(*ws):
    return np.stack([weight_tiles(w) for w in ws], axis=1).reshape(-1, P, ws[0].shape[0])


def kernel(x_prompt, x_sample, state_conv, cache_k, cache_v,
           ffn1_norm, ffn1_w_gate, ffn1_w_up, ffn1_w_down,
           mix_norm, conv_w_in, conv_w_dw, conv_w_out,
           attn_w_qkv, attn_w_o, attn_rel_bias,
           ffn2_norm, ffn2_w_gate, ffn2_w_up, ffn2_w_down,
           final_norm):
    import concourse.bacc as _bacc
    from concourse.bass_utils import run_bass_kernel_spmd as _run

    a = {n: np.asarray(v) for n, v in dict(
        x_prompt=x_prompt, x_sample=x_sample, state_conv=state_conv, cache_k=cache_k, cache_v=cache_v,
        ffn1_norm=ffn1_norm, ffn1_w_gate=ffn1_w_gate, ffn1_w_up=ffn1_w_up, ffn1_w_down=ffn1_w_down,
        mix_norm=mix_norm, conv_w_in=conv_w_in, conv_w_dw=conv_w_dw, conv_w_out=conv_w_out,
        attn_w_qkv=attn_w_qkv, attn_w_o=attn_w_o, attn_rel_bias=attn_rel_bias,
        ffn2_norm=ffn2_norm, ffn2_w_gate=ffn2_w_gate, ffn2_w_up=ffn2_w_up, ffn2_w_down=ffn2_w_down,
        final_norm=final_norm).items()}

    streams = {8: [], 6: []}
    for p in PHASES:
        if p.kind in ("up", "down"):
            layer, name = p.ffn // 2, f"ffn{p.ffn % 2 + 1}"
            first = sum(FFN_CHUNKS[:p.chunk]) * P
            part = slice(first, first + FFN_CHUNKS[p.chunk] * P)
            if p.kind == "up":
                w = interleaved(a[name + "_w_gate"][layer][:, part], a[name + "_w_up"][layer][:, part])
            else:
                w = weight_tiles(a[name + "_w_down"][layer][part])
        elif p.kind == "conv_in":
            b, c, h = np.split(a["conv_w_in"][0], 3, axis=1)
            w = interleaved(c, h, b)
        elif p.kind == "qkv":
            w = interleaved(*np.split(a["attn_w_qkv"][0], 3, axis=1))
        else:
            w = weight_tiles(a["conv_w_out" if p.kind == "conv_out" else "attn_w_o"][0])
        streams[p.k].append(w)

    def by_feature(v):
        return np.moveaxis(v.reshape(v.shape[:-1] + (DT, P)), -1, 0)

    tokens = np.concatenate([a["x_prompt"][0], a["x_sample"][0]], axis=0)
    norms = np.stack([a["ffn1_norm"][0], a["mix_norm"][0], a["ffn2_norm"][0],
                      a["ffn1_norm"][1], a["mix_norm"][1], a["ffn2_norm"][1], a["final_norm"]])
    rel = a["attn_rel_bias"][0][:, REL_CLIP - P + 1:]
    rel = np.pad(rel, ((0, 0), (0, EXT - rel.shape[1])), mode="edge")
    ins = {
        "x_t": tokens.T.reshape(DT, P, TOK),
        "w8": np.concatenate(streams[8]),
        "w6": np.concatenate(streams[6]),
        "gains": by_feature(norms),
        "conv_taps": by_feature(a["conv_w_dw"][0]),
        "conv_state": np.moveaxis(by_feature(a["state_conv"][0, 0]), 1, 2),
        "cache_kt": a["cache_k"][0, 0].reshape(PAST, D_MODEL).T.reshape(DT, P, PAST),
        "cache_v": a["cache_v"][0, 0].reshape(PAST, DT, P).transpose(1, 0, 2),
        "bias_ext": rel,
        "ident_in": np.eye(P, dtype=np.float32),
    }
    outs = {
        "y_t": (DT, P, TOK),
        "conv_out_state": (P, DT, 2 * CONV_PAD),
        "k_t": (DT, P, TOK),
        "v_t": (DT, P, TOK),
    }
    nc = _bacc.Bacc("TRN2", target_bir_lowering=False, num_devices=1)
    arrays, args = {}, {}
    for name, v in ins.items():
        arrays[name] = np.ascontiguousarray(v)
        args[name] = nc.dram_tensor(name, arrays[name].shape, F32, kind="ExternalInput").ap()
    for name, shape in outs.items():
        args[name] = nc.dram_tensor(name, shape, F32, kind="ExternalOutput").ap()
    streaming_conv_chunkattn_macaron(nc, **args)
    got = _run(nc, [arrays], core_ids=[0]).results[0]

    y = got["y_t"].reshape(D_MODEL, TOK).T
    k = got["k_t"].reshape(D_MODEL, TOK).T.reshape(TOK, HEADS, HEAD_DIM)
    v = got["v_t"].reshape(D_MODEL, TOK).T.reshape(TOK, HEADS, HEAD_DIM)
    state = got["conv_out_state"].transpose(2, 1, 0).reshape(2, CONV_PAD, D_MODEL)
    c = np.ascontiguousarray
    return (c(y[None, :SEQ]), c(y[None, SEQ:]), c(state[None, 0:1]), c(state[None, 1:2]),
            c(k[None, None, :SEQ]), c(v[None, None, :SEQ]), c(k[None, None, SEQ:]), c(v[None, None, SEQ:]))
```
